# Optimizing a Trainium2 kernel written in Bass

```python
import jax, jax.numpy as jnp
from jax import lax
import numpy as np

D_MODEL = 1024
BATCH = 1
SEQ = 512
DEPTH = 1

CHUNK = 64
Q_BLOCK = 128
SB_HEADS = 8
SB_HEAD_DIM = 64
SB_WIDTH = SB_HEADS * SB_HEAD_DIM
CA_HEADS = 8
CA_HEAD_DIM = 64
CA_WIDTH = CA_HEADS * CA_HEAD_DIM
CA_LEFT_CHUNKS = 8
CA_BAND = (CA_LEFT_CHUNKS + 1) * CHUNK
REL_CLIP = 256
N_BRANCH = 2
PROJ_WIDTH = 3 * SB_WIDTH + 3 * CA_WIDTH
N_EXPERTS = 32
TOP_K = 4
D_EXPERT = D_MODEL
SWIGLU_ALPHA = 1.702
SWIGLU_LIMIT = 7.0
MOE_BLOCK = 128
RMS_EPS = 1e-6
N_MOD = 6

kernel_name = 'hybrid_stickbreak_chunkattn_moe_block'

def rms_norm(x, g):
    xf = x.astype(jnp.float32)
    y = xf * lax.rsqrt(jnp.mean(xf * xf, axis=-1, keepdims=True) + RMS_EPS)
    return (y * g.astype(jnp.float32)).astype(x.dtype)

def to_heads(t, n_heads):
    b, s, w = t.shape
    return t.reshape(b, s, n_heads, w // n_heads).transpose(0, 2, 1, 3)

def from_heads(t):
    b, h, s, dh = t.shape
    return t.transpose(0, 2, 1, 3).reshape(b, s, h * dh)

def stick_breaking_attention(q, k, v):
    b, h, s, d = q.shape
    n_blk = s // Q_BLOCK
    scale = d ** -0.5
    q_blocks = q.reshape(b, h, n_blk, Q_BLOCK, d).transpose(2, 0, 1, 3, 4)
    key_pos = jnp.arange(s)

    def one_block(args):
        q_blk, blk = args
        z = jnp.einsum('bhqd,bhkd->bhqk', q_blk, k).astype(jnp.float32) * scale
        q_pos = blk * Q_BLOCK + jnp.arange(Q_BLOCK)
        causal = key_pos[None, :] < q_pos[:, None]
        sp = jnp.where(causal, jax.nn.softplus(z), 0.0)
        between = lax.cumsum(sp, axis=3, reverse=True) - sp
        a = jnp.where(causal, jnp.exp(jax.nn.log_sigmoid(z) - between), 0.0)
        return jnp.einsum('bhqk,bhkd->bhqd', a.astype(v.dtype), v)

    o = lax.map(one_block, (q_blocks, jnp.arange(n_blk)))
    return o.transpose(1, 2, 0, 3, 4).reshape(b, h, s, d)

def chunked_band_attention(q, k, v, rel_bias):
    b, h, s, d = q.shape
    n_chunk = s // CHUNK
    pad = CA_LEFT_CHUNKS * CHUNK
    scale = d ** -0.5
    kp = jnp.pad(k, ((0, 0), (0, 0), (pad, 0), (0, 0)))
    vp = jnp.pad(v, ((0, 0), (0, 0), (pad, 0), (0, 0)))
    band_idx = jnp.arange(n_chunk)[:, None] * CHUNK + jnp.arange(CA_BAND)[None, :]
    k_band = kp[:, :, band_idx]
    v_band = vp[:, :, band_idx]
    q_chunk = q.reshape(b, h, n_chunk, CHUNK, d)
    z = jnp.einsum('bhcqd,bhckd->bhcqk', q_chunk, k_band).astype(jnp.float32) * scale
    rel = pad + jnp.arange(CHUNK)[:, None] - jnp.arange(CA_BAND)[None, :]
    bias = rel_bias[:, jnp.clip(rel, -REL_CLIP, REL_CLIP) + REL_CLIP]
    z = z + bias[None, :, None, :, :].astype(jnp.float32)
    valid = band_idx >= pad
    z = jnp.where(valid[None, None, :, None, :], z, -jnp.inf)
    p = jax.nn.softmax(z, axis=-1)
    o = jnp.einsum('bhcqk,bhckd->bhcqd', p.astype(v.dtype), v_band)
    return o.reshape(b, h, s, d)

def clamped_swiglu(hh):
    gate, up = jnp.split(hh, 2, axis=-1)
    gate = jnp.minimum(gate, SWIGLU_LIMIT)
    up = jnp.clip(up, -SWIGLU_LIMIT, SWIGLU_LIMIT)
    return gate * jax.nn.sigmoid(SWIGLU_ALPHA * gate) * (up + 1.0)

def moe_ffn(h, w_router, b_router, w1, b1, w2, b2):
    n, d = h.shape
    logits = (h @ w_router + b_router).astype(jnp.float32)
    top_logit, top_e = lax.top_k(logits, TOP_K)
    top_w = jax.nn.softmax(top_logit, axis=-1)
    nk = n * TOP_K
    flat_e = top_e.reshape(nk)
    flat_tok = jnp.arange(nk, dtype=jnp.int32) // TOP_K
    flat_w = top_w.reshape(nk)
    order = jnp.argsort(flat_e)
    sorted_e = flat_e[order]
    counts = jnp.bincount(flat_e, length=N_EXPERTS)
    padded = (counts + MOE_BLOCK - 1) // MOE_BLOCK * MOE_BLOCK
    pad_end = jnp.cumsum(padded)
    pad_start = pad_end - padded
    grp_start = jnp.cumsum(counts) - counts
    dest = pad_start[sorted_e] + jnp.arange(nk) - grp_start[sorted_e]
    n_blocks = -(-nk // MOE_BLOCK) + N_EXPERTS
    rows = n_blocks * MOE_BLOCK
    row_tok = jnp.zeros((rows,), jnp.int32).at[dest].set(flat_tok[order])
    row_w = jnp.zeros((rows,), jnp.float32).at[dest].set(flat_w[order])
    block_e = jnp.minimum(
        jnp.searchsorted(pad_end, jnp.arange(n_blocks) * MOE_BLOCK, side='right'), N_EXPERTS - 1)
    xs = h[row_tok].reshape(n_blocks, MOE_BLOCK, d)

    def expert_block(args):
        xb, e = args
        hid = clamped_swiglu(xb @ w1[e] + b1[e])
        return hid @ w2[e] + b2[e]

    ys = lax.map(expert_block, (xs, block_e)).reshape(rows, d)
    out = jax.ops.segment_sum(ys.astype(jnp.float32) * row_w[:, None], row_tok, num_segments=n)
    return out.astype(h.dtype)

def setup_inputs(seed: int = 0) -> dict:
    key = jax.random.key(seed)
    ks = jax.random.split(key, 24)
    L, D, E, I = DEPTH, D_MODEL, N_EXPERTS, D_EXPERT
    nrm = lambda k, shape, s: jax.random.normal(k, shape, jnp.float32) * s
    return {
        'x': nrm(ks[0], (BATCH, SEQ, D), 1.0),
        'c': nrm(ks[1], (BATCH, D), 1.0),
        'w_ada': nrm(ks[2], (L, D, N_MOD * D), 0.25 * D ** -0.5),
        'b_ada': nrm(ks[3], (L, N_MOD * D), 0.02),
        'g_pre_mix': 1.0 + nrm(ks[4], (L, D), 0.05),
        'g_post_mix': 1.0 + nrm(ks[5], (L, D), 0.05),
        'w_in': nrm(ks[6], (L, D, PROJ_WIDTH), D ** -0.5),
        'rel_bias': nrm(ks[7], (L, CA_HEADS, 2 * REL_CLIP + 1), 0.5),
        'w_branch_sb': nrm(ks[8], (L, SB_WIDTH, D), SB_WIDTH ** -0.5),
        'w_branch_ca': nrm(ks[9], (L, CA_WIDTH, D), CA_WIDTH ** -0.5),
        'w_gate': nrm(ks[10], (L, D, N_BRANCH * D), D ** -0.5),
        'b_gate': nrm(ks[11], (L, N_BRANCH * D), 0.02),
        'w_out': nrm(ks[12], (L, D, D), D ** -0.5),
        'g_pre_ffn': 1.0 + nrm(ks[13], (L, D), 0.05),
        'g_post_ffn': 1.0 + nrm(ks[14], (L, D), 0.05),
        'w_router': nrm(ks[15], (L, D, E), D ** -0.5),
        'b_router': nrm(ks[16], (L, E), 0.01),
        'w_e1': nrm(ks[17], (L, E, D, 2 * I), D ** -0.5),
        'b_e1': nrm(ks[18], (L, E, 2 * I), 0.02),
        'w_e2': nrm(ks[19], (L, E, I, D), I ** -0.5),
        'b_e2': nrm(ks[20], (L, E, D), 0.02),
    }

def reference(x, c, w_ada, b_ada, g_pre_mix, g_post_mix, w_in, rel_bias, w_branch_sb, w_branch_ca,
              w_gate, b_gate, w_out, g_pre_ffn, g_post_ffn, w_router, b_router, w_e1, b_e1, w_e2, b_e2):
    b, s, d = x.shape
    for l in range(DEPTH):
        mod = (c @ w_ada[l] + b_ada[l])[:, None, :]
        sh_m, sc_m, gt_m, sh_f, sc_f, gt_f = jnp.split(mod, N_MOD, axis=-1)

        h = rms_norm(x, g_pre_mix[l]) * (1.0 + sc_m) + sh_m
        proj = h @ w_in[l]
        q_sb, k_sb, v_sb, q_ca, k_ca, v_ca = jnp.split(proj, 6, axis=-1)
        o_sb = stick_breaking_attention(to_heads(q_sb, SB_HEADS), to_heads(k_sb, SB_HEADS),
                                        to_heads(v_sb, SB_HEADS))
        o_ca = chunked_band_attention(to_heads(q_ca, CA_HEADS), to_heads(k_ca, CA_HEADS),
                                      to_heads(v_ca, CA_HEADS), rel_bias[l])
        y_sb = from_heads(o_sb) @ w_branch_sb[l]
        y_ca = from_heads(o_ca) @ w_branch_ca[l]
        g_sb, g_ca = jnp.split(jax.nn.sigmoid(h @ w_gate[l] + b_gate[l]), N_BRANCH, axis=-1)
        mixed = (g_sb * y_sb + g_ca * y_ca) @ w_out[l]
        x = x + gt_m * rms_norm(mixed, g_post_mix[l])

        h2 = rms_norm(x, g_pre_ffn[l]) * (1.0 + sc_f) + sh_f
        ff = moe_ffn(h2.reshape(b * s, d), w_router[l], b_router[l], w_e1[l], b_e1[l],
                     w_e2[l], b_e2[l]).reshape(b, s, d)
        x = x + gt_f * rms_norm(ff, g_post_ffn[l])
    return x


_drawn_inputs = setup_inputs


def setup_inputs(seed=0):
    import zlib

    import numpy as np

    out = dict(_drawn_inputs(seed))
    spreads = {}
    factors = {'b_gate': 8.0, 'g_post_ffn': 5.048, 'b_router': 3.111, 'b_e1': 8.0, 'b_e2': 8.0}
    for name, (base, spread) in spreads.items():
        noise = np.random.default_rng([zlib.crc32(name.encode()), seed]).standard_normal(out[name].shape)
        drawn = base * np.exp(spread * noise) if base else spread * noise
        out[name] = __import__('jax').numpy.asarray(drawn.astype(out[name].dtype))
    for name, factor in factors.items():
        out[name] = (out[name] * factor).astype(out[name].dtype)
    return out
```

```python
from contextlib import ExitStack

import concourse.bass as bass
from concourse import mybir

ALU = mybir.AluOpType
ACT = mybir.ActivationFunctionType
AX = mybir.AxisListType
F32 = mybir.dt.float32
F32R = mybir.dt.float32r
BF16 = mybir.dt.bfloat16
I32 = mybir.dt.int32

P = 128
D = 1024
S = 512
KT = D // P
NT = S // P
HEADS = 8
DH = 64
PAIRS = HEADS // 2
W = HEADS * DH
REL_CLIP = 256
CHUNK = 64
E = 32
TOPK = 4
EPS = 1e-6
SLOTS = P
MAXB = E + (S * TOPK - E) // SLOTS + 1
NEG = -1.0e30
LIMIT = 7.0
SIG_ALPHA = 1.702

CW = 2048
NRAW = 4
NSPL = 3
ERAW = 6
ESPL = 4
BW = 2 * D + D

SOFF = [0, 512, 1024, 896]
SWID = [512, 384, 256, 128]
QOFF = SOFF[::-1]
QWID = SWID[::-1]
SC = 1280

JOBS = [("q_sb", "w_in", 0, KT, True), ("k_sb", "w_in", W, KT, True), ("v_sb", "w_in", 2 * W, KT, False),
        ("q_ca", "w_in", 3 * W, KT, True), ("k_ca", "w_in", 4 * W, KT, True), ("v_ca", "w_in", 5 * W, KT, False)]
for _g in range(2):
    JOBS += [("gate_sb", "w_gate", 512 * _g, KT, True), ("y_sb", "w_branch_sb", 512 * _g, NT, True),
             ("gate_ca", "w_gate", D + 512 * _g, KT, True), ("y_ca", "w_branch_ca", 512 * _g, NT, True)]
JOBS += [("out", "w_out", 0, KT, False), ("out", "w_out", 512, KT, False)]
N_PROJ = 6
N_MERGE = 8

STREAM = [("ada", 0, k) for k in range(KT)]
_later = [("ada", q, k) for q in (1, 2) for k in range(KT)]
for _j, (_n, _w, _c, _kt, _t) in enumerate(JOBS):
    STREAM += [("w", _j, c) for c in range(_kt // 4)]
    if _j < N_PROJ:
        _take = 3 if _j < 4 else 2
        STREAM += _later[:_take]
        _later = _later[_take:]
N_RAW1 = len(STREAM)
N_SPL1 = sum(1 for s in STREAM if s[0] == "w")
assert N_RAW1 % NRAW == 0 and not _later
W1C = D * 2 * D // (P * CW)
W2C = D * D // (P * CW)
EC = W1C + W2C
N_ADA_END = max(n for n, s in enumerate(STREAM) if s[0] == "ada") + 1
assert EC % ERAW == 0 and EC % ESPL == 0
SPL_ORDER = [(N_SPL1 + i) % NSPL for i in range(NSPL)] + list(range(NSPL, ESPL))


def raw_slot(q):
    return q % ERAW


def spl_slot(q):
    return SPL_ORDER[q % ESPL]


def raw_use(i, q):
    before = N_RAW1 // NRAW if raw_slot(q) < NRAW else 0
    return i * (16 * EC // ERAW) + 16 * (before + q // ERAW + 1)


def read_up_to(i, q):
    return i * EC + (N_RAW1 + q + 1)


def used_up_to(i, q):
    return i * EC + (N_SPL1 + q + 1)


def job_chunks(j):
    return sum(job[3] // 4 for job in JOBS[:j])


def raw_chunks(j):
    return [(n, s) for n, s in enumerate(STREAM) if s[0] == "w" and s[1] == j]


def row_ap(t, offset, n, parts=P):
    return bass.AP(t.tensor, offset, [[0, parts], [1, n]])


def trunk_layer(nc, x, c, w_ada, b_ada, g_pre_mix, g_post_mix, w_in, rel_tiles, w_branch_sb, w_branch_ca,
                w_gate, b_gate, w_out, g_pre_ffn, g_post_ffn, w_router, b_router, w_e1, b_e1, w_e2, b_e2, out):
    ctx = ExitStack()
    with ctx:
        base = [(nc.sbuf_base + 63) // 64 * 64]

        def at(name, shape, dt, offset):
            return nc.alloc_sbuf_tensor_at(name, shape, dt, offset=offset)

        def bytes_of(shape):
            n = 4
            for s in shape[1:]:
                n *= s
            return (n + 63) // 64 * 64

        def keep(name, shape, dt=F32):
            t = at(name, shape, dt, base[0])
            base[0] += bytes_of(shape)
            return t

        raw = keep("raw", [P, NRAW, CW])
        w_hi = keep("w_hi", [P, NSPL, CW], F32R)
        w_lo = keep("w_lo", [P, NSPL, CW], F32R)
        ident = keep("ident", [P, P])
        ident_b = keep("ident_b", [P, P], BF16)
        mask_b = keep("mask_b", [P, P], BF16)
        ones = keep("ones", [P, P])
        tri = keep("tri", [P, P])
        neg_tri = keep("neg_tri", [P, P], F32R)
        neg_ones = keep("neg_ones", [P, P], F32R)
        ones_r = keep("ones_r", [2, P], F32R)
        tri_f = keep("tri_f", [P, P])
        c_col = keep("c_col", [P, KT])
        bg_col = keep("bg_col", [P, 2 * KT])
        small = keep("small", [P, 96])
        w4 = keep("w4", [P, NT, TOPK])
        dest4 = keep("dest4", [P, NT, TOPK], I32)
        slot_tok = keep("slot_tok", [P, MAXB], I32)
        idx_now = keep("idx_now", [P, 1], I32)
        expert_of = keep("expert_of", [1, MAXB + 1], I32)

        arena = base[0]
        limit = 229344

        class Region:

            def __init__(self, start):
                self.pos = start

            def __call__(self, name, shape, dt=F32):
                t = at(name, shape, dt, self.pos)
                self.pos += bytes_of(shape)
                assert self.pos <= limit, (name, self.pos)
                return t

        B = Region(arena)
        hT_hi = B("hT_hi", [P, KT, S], F32R)
        hT_lo = B("hT_lo", [P, KT, S], F32R)
        c0 = B.pos
        C = Region(c0)
        q_sb = C("q_sb", [P, PAIRS, S])
        k_sb = C("k_sb", [P, PAIRS, S])
        v_sb = C("v_sb", [P, NT, W])
        q_ca = C("q_ca", [P, PAIRS, S])
        k_ca = C("k_ca", [P, PAIRS, S])
        v_ca = C("v_ca", [P, NT, W])
        d0 = C.pos
        A = Region(c0)
        x_in = A("x_in", [P, NT, D])
        junk = A("junk", [P, D])
        scale1 = A("scale1", [P, D])
        shift1 = A("shift1", [P, D])
        h_rows = A("h_rows", [P, 2, D])
        bias_in = A("bias_in", [E, BW])
        assert A.pos <= d0
        bias_hi = at("bias_hi", [E, BW], F32R, arena)
        bias_lo = at("bias_lo", [E, BW], F32R, arena + 4 * BW)
        Dm = Region(d0)
        mod_acc = Dm("mod_acc", [P, 3, CW])
        mod_row = Dm("mod_row", [1, 2, CW])
        Da = Region(d0)
        soft = Da("soft", [P, SC])
        sp = Da("sp", [P, SC])
        sp_hi = Da("sp_hi", [P, SC], F32R)
        sp_lo = Da("sp_lo", [P, SC], F32R)
        stick = Da("stick", [P, SC])
        zb = Da("zb", [P, SC])
        pT = Da("pT", [P, SC])
        rel = Da("rel", [P, 2, S])
        o_sb_hi = at("o_sb_hi", [P, PAIRS, S], F32R, c0 + 8 * 1024)
        o_sb_lo = at("o_sb_lo", [P, PAIRS, S], F32R, c0 + 16 * 1024)
        o_ca_hi = at("o_ca_hi", [P, PAIRS, S], F32R, c0 + 32 * 1024)
        o_ca_lo = at("o_ca_lo", [P, PAIRS, S], F32R, c0 + 40 * 1024)
        Dg = Region(d0)
        gates = Dg("gates", [P, 4, S])
        mix = Dg("mix", [P, KT, S])
        Z = Region(c0)
        x1 = Z("x1", [P, NT, D])
        F = Region(Z.pos)
        gate_post = F("gate_post", [P, D])
        scale2 = F("scale2", [P, D])
        shift2 = F("shift2", [P, D])
        g_row = F("g_row", [P, 2, D])
        h2 = F("h2", [P, NT, D])
        post = F("post", [P, D])
        junk2 = F("junk2", [P, D])
        h2T = at("h2T", [P, KT, S], F32, arena)
        R = Region(arena + 16 * 1024)
        wr = R("wr", [P, KT, E])
        br = R("br", [1, E])
        logit = R("logit", [P, NT, E])
        top8 = R("top8", [P, NT, 8])
        r_gt = R("r_gt", [P, NT, E])
        r_eq = R("r_eq", [P, NT, E])
        r_ceq = R("r_ceq", [P, NT, E])
        r_mask = R("r_mask", [P, NT, E])
        r_pos = R("r_pos", [P, NT, E])
        r_w = R("r_w", [P, NT, E])
        r_rank = R("r_rank", [P, NT, E])
        r_blk = R("r_blk", [P, NT, E])
        r_slot = R("r_slot", [P, NT, E])
        r_t1 = R("r_t1", [P, NT, E])
        r_t2 = R("r_t2", [P, NT, E])
        r_sum = R("r_sum", [P, NT, E])
        iota_e = R("iota_e", [P, E])
        iota_r = R("iota_r", [P, P])
        iota_n = R("iota_n", [P, MAXB])
        tok_id = R("tok_id", [P, NT])
        over = R("over", [P, 4, E])
        slot4 = R("slot4", [P, NT, TOPK])
        blk4 = R("blk4", [P, NT, TOPK])
        d4f = R("d4f", [P, NT, TOPK])
        hot_r = R("hot_r", [P, 2, P])
        hot_n = R("hot_n", [P, 2, MAXB])
        ov_m = R("ov_m", [1, MAXB - E, E])
        exp_f = R("exp_f", [1, MAXB + 1])
        assert R.pos <= c0
        raw_more = at("raw_more", [P, ERAW - NRAW, CW], F32, F.pos)
        hi_more = at("hi_more", [P, ESPL - NSPL, CW], F32R, arena + 8192)
        lo_more = at("lo_more", [P, ESPL - NSPL, CW], F32R, arena + 16384)
        assert F.pos + (ERAW - NRAW) * CW * 4 <= limit and arena + 24576 <= c0 and ESPL == NSPL + 1
        raws = [raw[:, i, :] for i in range(NRAW)] + [raw_more[:, i, :] for i in range(ERAW - NRAW)]
        his = [w_hi[:, i, :] for i in range(NSPL)] + [hi_more[:, i, :] for i in range(ESPL - NSPL)]
        los = [w_lo[:, i, :] for i in range(NSPL)] + [lo_more[:, i, :] for i in range(ESPL - NSPL)]
        M = Region(Z.pos)
        x_rows = M("x_rows", [P, D])
        xT_hi = M("xT_hi", [P, KT, P], F32R)
        xT_lo = M("xT_lo", [P, KT, P], F32R)
        gate_c = M("gate_c", [P, D])
        up_c = M("up_c", [P, D])
        sig = M("sig", [P, D])
        hid = M("hid", [P, D])
        y_out = M("y_out", [P, D])
        hidT_hi = at("hidT_hi", [P, KT, P], F32R, arena)
        hidT_lo = at("hidT_lo", [P, KT, P], F32R, arena + 4096)
        brow1 = M("brow1", [2, 2 * D], F32R)
        brow2 = M("brow2", [2, D], F32R)
        assert M.pos <= F.pos
        gate_end = at("gate_end", [P, D], F32, F.pos + (ERAW - NRAW) * CW * 4)
        g_end = at("g_end", [P, D], F32, F.pos + (ERAW - NRAW) * CW * 4 + 4096)
        ring0 = (nc.sbuf_base + 63) // 64 * 64
        g_buf = at("g_buf", [P, NT * TOPK, D], F32, ring0)
        T = Region(Z.pos)
        ff = T("ff", [P, NT, D])
        ff_junk = T("ff_junk", [P, D])
        o_rows = T("o_rows", [P, NT, D])
        assert NT * TOPK * D * 4 <= (NRAW + 2 * NSPL) * CW * 4

        ps = ctx.enter_context(nc.psum_tensor("ps", [P, 8, 512], F32))
        psf = ps[:, :, :].rearrange("p b n -> p (b n)")

        mod_d = nc.dram_tensor("mod_rows", (1, 6 * D), F32, kind="Internal").ap()
        bias_d = nc.dram_tensor("bias_parts", (2, E, BW), F32, kind="Internal").ap()
        h2_d = nc.dram_tensor("h2_rows", (S, D), F32, kind="Internal").ap()
        ys_d = nc.dram_tensor("expert_rows", (MAXB * SLOTS, D), F32, kind="Internal").ap()

        def sem(name):
            return ctx.enter_context(nc.semaphore(name))

        raw_full = [sem(f"raw_full{i}") for i in range(ERAW)]
        chunk_read = sem("chunk_read")
        hi_ready = sem("hi_ready")
        lo_ready = sem("lo_ready")
        chunk_used = sem("chunk_used")
        small_in = sem("small_in")
        x_loaded = sem("x_loaded")
        g1_in = sem("g1_in")
        bias_loaded = sem("bias_loaded")
        b_row_in = sem("b_row_in")
        consts = sem("consts")
        pool_step = sem("pool_step")
        passed = sem("passed")
        const_r = sem("const_r")
        dve_step = sem("dve_step")
        act_step = sem("act_step")
        mod_zero = sem("mod_zero")
        mod_summed = sem("mod_summed")
        mod_out = sem("mod_out")
        mod_taken = sem("mod_taken")
        mod_stored = sem("mod_stored")
        squares = sem("squares")
        mean_sq = sem("mean_sq")
        rooted = sem("rooted")
        h_ready = sem("h_ready")
        h_turned = sem("h_turned")
        hT_hi_ok = sem("hT_hi_ok")
        hT_lo_ok = sem("hT_lo_ok")
        bias_hi_ok = sem("bias_hi_ok")
        bias_lo_ok = sem("bias_lo_ok")
        bias_stored = sem("bias_stored")
        proj_taken = sem("proj_taken")
        gate_taken = sem("gate_taken")
        y_taken = sem("y_taken")
        mix_ok = sem("mix_ok")
        o_hi_ok = sem("o_hi_ok")
        o_lo_ok = sem("o_lo_ok")
        mix_hi_ok = sem("mix_hi_ok")
        mix_lo_ok = sem("mix_lo_ok")
        rel_in = [sem("rel_in0"), sem("rel_in1")]
        rel_used = sem("rel_used")
        rel_masked = sem("rel_masked")
        zs_ok = sem("zs_ok")
        zc_ok = sem("zc_ok")
        soft_ok = sem("soft_ok")
        sp_ok = sem("sp_ok")
        sp_hi_ok = sem("sp_hi_ok")
        sp_lo_ok = sem("sp_lo_ok")
        stick_ok = sem("stick_ok")
        a_ok = sem("a_ok")
        zb_ok = sem("zb_ok")
        exp_ok = sem("exp_ok")
        p_ok = sem("p_ok")
        p_turned = sem("p_turned")
        pT_ok = sem("pT_ok")
        os_ok = sem("os_ok")
        oc_ok = sem("oc_ok")
        os_taken = sem("os_taken")
        oc_taken = sem("oc_taken")
        post_in = sem("post_in")
        x_again = sem("x_again")
        x1_ok = sem("x1_ok")
        h2_ok = sem("h2_ok")
        h2_stored = sem("h2_stored")
        h2_turned = sem("h2_turned")
        h2T_ok = sem("h2T_ok")
        router_in = sem("router_in")
        logits_ok = sem("logits_ok")
        top_ok = sem("top_ok")
        top_exp = sem("top_exp")
        mask_ok = sem("mask_ok")
        rank_ok = sem("rank_ok")
        hot_ok = sem("hot_ok")
        hot_used = sem("hot_used")
        table_ok = sem("table_ok")
        idx_ok = sem("idx_ok")
        x_gathered = sem("x_gathered")
        x_turned = sem("x_turned")
        xT_hi_ok = sem("xT_hi_ok")
        xT_lo_ok = sem("xT_lo_ok")
        b1_in = sem("b1_in")
        b1_used = sem("b1_used")
        b2_in = sem("b2_in")
        b2_used = sem("b2_used")
        gate_ok = sem("gate_ok")
        up_ok = sem("up_ok")
        sg_ok = sem("sg_ok")
        ug_ok = sem("ug_ok")
        hid_ok = sem("hid_ok")
        hid_turned = sem("hid_turned")
        hidT_hi_ok = sem("hidT_hi_ok")
        hidT_lo_ok = sem("hidT_lo_ok")
        y_ok = sem("y_ok")
        y_stored = sem("y_stored")
        g_in = [sem(f"g_in{t}") for t in range(NT)]
        ys_filled = sem("ys_filled")
        end_in = sem("end_in")
        ff_ok = sem("ff_ok")
        normed = sem("normed")
        out_ok = sem("out_ok")
        out_stored = sem("out_stored")

        block = ctx.enter_context(nc.Block())

        weights = {"w_in": w_in[0], "w_gate": w_gate[0], "w_branch_sb": w_branch_sb[0],
                   "w_branch_ca": w_branch_ca[0], "w_out": w_out[0]}

        def mixed(t):
            return ps[:, :, :].rearrange("p (h t) n -> p t h n", h=2)[:, t]

        def turned_lo(dve, t):
            dve.wait_ge(hT_hi_ok, t + 1)
            dve.tensor_tensor(hT_lo[:, :, t * P:(t + 1) * P],
                              psf[:, (t % 2) * 1024:(t % 2) * 1024 + 1024].rearrange("p (k n) -> p k n", k=KT),
                              hT_hi[:, :, t * P:(t + 1) * P].bitcast(F32), ALU.subtract).then_inc(hT_lo_ok, 1)

        @block.sync
        def _(sp_):
            sp_.dma_start(c_col[:, :], c[0].rearrange("(k p) -> p k", p=P),
                          allow_slow_non_contiguous=True).then_inc(small_in, 16)
            sp_.dma_start(bg_col[:, :], b_gate[0].rearrange("(k p) -> p k", p=P),
                          allow_slow_non_contiguous=True).then_inc(small_in, 16)
            for n, item in enumerate(STREAM):
                if n >= NRAW:
                    sp_.wait_ge(chunk_read, n - NRAW + 1)
                slot = raw[:, n % NRAW, :]
                if item[0] == "ada":
                    _, q, k = item
                    src = w_ada[0, k * P:(k + 1) * P, q * CW:(q + 1) * CW]
                else:
                    _, j, half = item
                    _, wname, col, _, _ = JOBS[j]
                    src = weights[wname][half * 512:(half + 1) * 512, col:col + 512].rearrange(
                        "(k p) n -> p k n", p=P)
                    slot = slot.rearrange("p (k n) -> p k n", k=4)
                sp_.dma_start(slot, src).then_inc(raw_full[n % NRAW], 16)

            def load(i, q, src, k):
                slot = raw_slot(q)
                if isinstance(i, int) and NRAW <= q < ERAW:
                    sp_.wait_ge(chunk_used, job_chunks(N_PROJ + N_MERGE))
                    sp_.wait_ge(mix_lo_ok, 2)
                else:
                    sp_.wait_ge(chunk_read, read_up_to(i, q - (NRAW if isinstance(i, int) and q < NRAW else ERAW)))
                dst = raws[slot] if k == 1 else raws[slot].rearrange("p (k n) -> p k n", k=k)
                sp_.dma_start(dst, src).then_inc(raw_full[slot], 16)

            def w1_rows(e, c_):
                return w_e1[0, bass.ds(e, 1), c_ * P:(c_ + 1) * P, :].rearrange("e p n -> p (e n)")

            def w2_rows(e, c_):
                return w_e2[0, bass.ds(e, 1), c_ * 2 * P:(c_ + 1) * 2 * P, :].rearrange("e (k p) n -> p (e k) n", p=P)

            for c_ in range(W1C):
                load(0, c_, w_e1[0, 0, c_ * P:(c_ + 1) * P, :], 1)
            sp_.wait_ge(table_ok, 1)
            n_mid = sp_.value_load(expert_of[0:1, MAXB:MAXB + 1], min_val=E - 2, max_val=MAXB - 3)
            nblk = n_mid + 2
            with sp_.Fori(1, nblk) as i:
                e_now = sp_.value_load(expert_of[0:1, bass.ds(i, 1)], min_val=0, max_val=E - 1)
                for c_ in range(W1C):
                    load(i, c_ - W2C, w1_rows(e_now, c_), 1)
                e_was = sp_.value_load(expert_of[0:1, bass.ds(i - 1, 1)], min_val=0, max_val=E - 1)
                for c_ in range(W2C):
                    load(i, c_ + W1C - W2C, w2_rows(e_was, c_), 2)
            e_last = sp_.value_load(expert_of[0:1, bass.ds(n_mid + 1, 1)], min_val=0, max_val=E - 1)
            for c_ in range(W2C):
                load(nblk, c_ - W2C, w2_rows(e_last, c_), 2)

        @block.gpsimd
        def _(pool):
            n_step = [0]

            def step(ins):
                n_step[0] += 1
                ins.then_inc(pool_step, 1)
                pool.wait_ge(pool_step, n_step[0])

            xr = x[0].rearrange("(t p) d -> p t d", p=P)
            for t in range(NT):
                pool.dma_start(x_in[:, t, :], xr[:, t, :]).then_inc(x_loaded, 16)
            pool.wait_ge(mod_zero, 1)
            pool.dma_start(mod_acc[0:1, :, :], b_ada.rearrange("o (q n) -> o q n", n=CW)).then_inc(b_row_in, 16)
            pool.dma_start(junk[:, :], row_ap(g_pre_mix, 0, D)).then_inc(g1_in, 16)
            pool.dma_start(bias_in[:, 0:2 * D], b_e1[0]).then_inc(bias_loaded, 16)
            pool.dma_start(bias_in[:, 2 * D:BW], b_e2[0]).then_inc(bias_loaded, 16)

            step(pool.memset(ones[:, :], 1.0))
            step(pool.memset(tri_f[:, :], 0.0))
            pool.affine_select(out=ident[:, :], in_=tri_f[:, :], compare_op=ALU.not_equal, fill=1.0, base=0,
                               pattern=[[-1, P]], channel_multiplier=1).then_inc(consts, 1)
            pool.affine_select(out=ident_b[:, :], in_=tri_f[:, :], compare_op=ALU.not_equal, fill=1.0, base=0,
                               pattern=[[-1, P]], channel_multiplier=1).then_inc(consts, 1)
            pool.affine_select(out=tri[:, :], in_=tri_f[:, :], compare_op=ALU.is_ge, fill=1.0, base=0,
                               pattern=[[-1, P]], channel_multiplier=1).then_inc(consts, 1)
            pool.affine_select(out=mask_b[:, :], in_=tri_f[:, :], compare_op=ALU.is_gt, fill=NEG, base=0,
                               pattern=[[1, P]], channel_multiplier=-1).then_inc(consts, 1)
            pool.wait_ge(consts, 4)
            pool.affine_select(out=tri_f[:, :], in_=tri_f[:, :], compare_op=ALU.is_gt, fill=-1.0, base=0,
                               pattern=[[1, P]], channel_multiplier=-1).then_inc(consts, 1)

            pool.wait_ge(bias_hi_ok, 1)
            pool.dma_start(bias_d[0], bias_hi[:, :].bitcast(F32)).then_inc(bias_stored, 16)
            pool.wait_ge(bias_lo_ok, 1)
            pool.dma_start(bias_d[1], bias_lo[:, :].bitcast(F32)).then_inc(bias_stored, 16)

            for q in range((MAXB - E) * SLOTS // S):
                pool.dma_start(ys_d[E * SLOTS + q * S:E * SLOTS + (q + 1) * S, :], x[0]).then_inc(ys_filled, 16)

            for h in range(HEADS):
                if h == 0:
                    pool.wait_ge(mod_stored, 32)
                if h >= 2:
                    pool.wait_ge(rel_used, h - 1)
                pool.dma_start(rel[:, h % 2, :], rel_tiles[h]).then_inc(rel_in[h % 2], 16)
                pool.wait_ge(rel_in[h % 2], 16 * (h // 2 + 1))
                pool.memset(rel[0:CHUNK, h % 2, S - CHUNK:S], NEG).then_inc(rel_masked, 1)

            pool.wait_ge(chunk_used, job_chunks(N_PROJ + N_MERGE))
            pool.dma_start(gate_post[:, :], row_ap(mod_d, 2 * D, D)).then_inc(post_in, 16)
            pool.dma_start(shift2[:, :], row_ap(mod_d, 3 * D, D)).then_inc(post_in, 16)
            pool.dma_start(scale2[:, :], row_ap(mod_d, 4 * D, D)).then_inc(post_in, 16)
            pool.dma_start(g_row[:, 0, :], row_ap(g_post_mix, 0, D)).then_inc(post_in, 16)
            pool.dma_start(g_row[:, 1, :], row_ap(g_pre_ffn, 0, D)).then_inc(post_in, 16)
            for t in range(NT):
                pool.dma_start(x1[:, t, :], xr[:, t, :]).then_inc(x_again, 16)
            pool.wait_ge(chunk_used, N_SPL1)
            pool.dma_start(wr[:, :, :], w_router[0].rearrange("(k p) e -> p k e", p=P)).then_inc(router_in, 16)
            pool.dma_start(br[:, :], b_router[0:1, :]).then_inc(router_in, 16)
            pool.iota(iota_e[:, :], pattern=[[1, E]], base=0, channel_multiplier=0,
                      allow_small_or_imprecise_dtypes=True).then_inc(consts, 1)
            pool.iota(iota_r[:, :], pattern=[[1, P]], base=0, channel_multiplier=0,
                      allow_small_or_imprecise_dtypes=True).then_inc(consts, 1)
            pool.iota(iota_n[:, :], pattern=[[1, MAXB]], base=0, channel_multiplier=0,
                      allow_small_or_imprecise_dtypes=True).then_inc(consts, 1)
            pool.iota(tok_id[:, :], pattern=[[P, NT]], base=0, channel_multiplier=1,
                      allow_small_or_imprecise_dtypes=True).then_inc(consts, 1)
            for t in range(NT):
                pool.wait_ge(h2_ok, t + 1)
                pool.dma_start(h2_d[t * P:(t + 1) * P, :], h2[:, t, :]).then_inc(h2_stored, 16)

            pool.dma_start(gate_end[:, :], row_ap(mod_d, 5 * D, D)).then_inc(end_in, 16)
            pool.dma_start(g_end[:, :], row_ap(g_post_ffn, 0, D)).then_inc(end_in, 16)

            pool.wait_ge(table_ok, 1)
            pool.wait_ge(h2_stored, 16 * NT)
            pool.wait_ge(h2_turned, NT)
            pool.wait_ge(bias_stored, 32)
            n_mid = pool.value_load(expert_of[0:1, MAXB:MAXB + 1], min_val=E - 2, max_val=MAXB - 3)
            nblk = n_mid + 2

            def gather_x(b):
                pool.tensor_copy(idx_now[:, :], slot_tok[:, b:b + 1] if isinstance(b, int)
                                 else slot_tok[:, bass.ds(b, 1)]).then_inc(idx_ok, 1)
                pool.wait_ge(idx_ok, b + 1)
                pool.sem_inc(passed, 1)
                pool.indirect_dma_start(
                    out=x_rows[:, :], out_offset=None, in_=h2_d[:, :],
                    in_offset=bass.IndirectOffsetOnAxis(ap=idx_now[:, 0:1], axis=0)).then_inc(x_gathered, 16)

            def load_b1(e):
                pool.dma_start(brow1[:, :].bitcast(F32).rearrange("q (o n) -> q o n", o=1),
                               bias_d[:, bass.ds(e, 1), 0:2 * D]).then_inc(b1_in, 16)

            def load_b2(e):
                pool.dma_start(brow2[:, :].bitcast(F32).rearrange("q (o n) -> q o n", o=1),
                               bias_d[:, bass.ds(e, 1), 2 * D:BW]).then_inc(b2_in, 16)

            gather_x(0)
            load_b1(0)
            pool.wait_ge(x_turned, 1)
            gather_x(1)
            pool.wait_ge(b1_used, 1)
            load_b1(1)
            load_b2(0)
            with pool.Fori(1, nblk) as i:
                pool.wait_ge(x_turned, i + 1)
                gather_x(i + 1)
                e_next = pool.value_load(expert_of[0:1, bass.ds(i + 1, 1)], min_val=0, max_val=E - 1)
                pool.wait_ge(b1_used, i + 1)
                load_b1(e_next)
                e_now = pool.value_load(expert_of[0:1, bass.ds(i, 1)], min_val=0, max_val=E - 1)
                pool.wait_ge(b2_used, i)
                load_b2(e_now)

            pool.wait_ge(y_stored, nblk * 16)
            pool.sem_inc(passed, 1)
            for t in range(NT):
                for k in range(TOPK):
                    pool.indirect_dma_start(
                        out=g_buf[:, t * TOPK + k, :], out_offset=None, in_=ys_d[:, :],
                        in_offset=bass.IndirectOffsetOnAxis(ap=dest4[:, t, k:k + 1], axis=0)).then_inc(g_in[t], 16)
            orow = out[0].rearrange("(t p) d -> p t d", p=P)
            for t in range(NT):
                pool.wait_ge(normed, t + 1)
                pool.tensor_tensor(o_rows[:, t, :], o_rows[:, t, :], x1[:, t, :], ALU.add).then_inc(out_ok, 1)
                pool.wait_ge(out_ok, t + 1)
                pool.dma_start(orow[:, t, :], o_rows[:, t, :]).then_inc(out_stored, 16)
            pool.wait_ge(out_stored, 16 * NT)

        @block.scalar
        def _(act):
            n_step = [0]

            def step(ins):
                n_step[0] += 1
                ins.then_inc(act_step, 1)
                act.wait_ge(act_step, n_step[0])

            def split_hi(n, m, raw_slot, raw_count, spl_slot):
                act.wait_ge(raw_full[raw_slot], raw_count)
                if not isinstance(m, int) or m >= NSPL:
                    act.wait_ge(chunk_used, m - NSPL + 1)
                act.copy(w_hi[:, spl_slot, :], raw[:, raw_slot, :]).then_inc(hi_ready, 1)

            def split_job(j):
                for q, (n, item) in enumerate(raw_chunks(j)):
                    m = job_chunks(j) + q
                    split_hi(n, m, n % NRAW, 16 * (n // NRAW + 1), m % NSPL)

            act.wait_ge(consts, 5)
            act.copy(neg_tri[:, :], tri_f[:, :]).then_inc(const_r, 1)
            act.mul(neg_ones[:, :], ones[:, :], -1.0).then_inc(const_r, 1)
            act.copy(ones_r[:, :], ones[0:2, :]).then_inc(const_r, 1)

            act.wait_ge(x_loaded, 16 * NT)
            for t in range(NT):
                if t >= 1:
                    act.wait_ge(squares, t)
                act.activation(h_rows[:, 0, :], x_in[:, t, :], ACT.Square,
                               accum_out=small[:, t:t + 1]).then_inc(squares, 1)
            act.wait_ge(bias_loaded, 32)
            act.copy(bias_hi[:, :], bias_in[:, :]).then_inc(bias_hi_ok, 1)
            act.wait_ge(mean_sq, 1)
            act.activation(small[:, 8:12], small[:, 4:8], ACT.Sqrt).then_inc(rooted, 1)
            split_job(0)
            act.wait_ge(bias_stored, 32)
            for t in range(NT):
                act.wait_ge(h_turned, t + 1)
                act.copy(hT_hi[:, :, t * P:(t + 1) * P],
                         psf[:, (t % 2) * 1024:(t % 2) * 1024 + 1024].rearrange("p (k n) -> p k n", k=KT)
                         ).then_inc(hT_hi_ok, 1)

            for j in range(N_PROJ):
                split_job(j + 1)
                act.wait_ge(chunk_used, job_chunks(j + 1))
                dst = [q_sb, k_sb, v_sb, q_ca, k_ca, v_ca][j]
                src = ps[:, 4 * (j % 2):4 * (j % 2) + 4, :]
                if j % 3 == 0:
                    act.mul(dst[:, :, :], src, DH ** -0.5).then_inc(proj_taken, 1)
                else:
                    act.copy(dst[:, :, :], src).then_inc(proj_taken, 1)
            for q in (1, 2):
                act.wait_ge(mod_out, q + 1)
                act.copy(mod_row[0:1, q - 1, :], psf[0:1, (q - 1) * CW:q * CW]).then_inc(mod_taken, 1)
                act.wait_ge(mod_taken, q)
                act.dma_start(mod_d[0:1, q * CW:(q + 1) * CW], mod_row[0:1, q - 1, :]).then_inc(mod_stored, 16)

            for h in range(HEADS):
                act.wait_ge(zs_ok, h + 1)
                if h >= 1:
                    act.wait_ge(sp_ok, h)
                step(act.activation(soft[:, :], psf[:, 0:SC], ACT.Abs))
                step(act.activation(soft[:, :], soft[:, :], ACT.Exp, scale=-1.0))
                act.activation(soft[:, :], soft[:, :], ACT.Ln, bias=1.0).then_inc(soft_ok, 1)
                act.wait_ge(zb_ok, h + 1)
                for i in range(NT):
                    zq = zb[:, QOFF[i]:QOFF[i] + QWID[i]]
                    ins = act.activation(zq, zq, ACT.Exp, bias=small[:, 84 + i:85 + i],
                                         accum_out=small[:, 88 + i:89 + i])
                ins.then_inc(exp_ok, 1)
                act.wait_ge(sp_ok, h + 1)
                if h >= 1:
                    act.wait_ge(stick_ok, h)
                act.copy(sp_hi[:, :], sp[:, :]).then_inc(sp_hi_ok, 1)
                act.wait_ge(stick_ok, h + 1)
                if h >= 1:
                    act.wait_ge(os_ok, h)
                act.activation(stick[:, :], psf[:, 0:SC], ACT.Exp).then_inc(a_ok, 1)
                act.wait_ge(p_turned, h + 1)
                if h >= 1:
                    act.wait_ge(oc_ok, h)
                act.copy(pT[:, :], psf[:, 3 * 512:3 * 512 + SC]).then_inc(pT_ok, 1)
                r, p = DH * (h % 2), h // 2
                act.wait_ge(os_ok, h + 1)
                act.copy(q_sb[r:r + DH, p, :], ps[r:r + DH, 6, :]).then_inc(os_taken, 1)
                act.wait_ge(oc_ok, h + 1)
                act.copy(q_ca[r:r + DH, p, :], ps[r:r + DH, 7, :]).then_inc(oc_taken, 1)
            act.wait_ge(os_taken, HEADS)
            act.wait_ge(oc_taken, HEADS)
            act.copy(o_sb_hi[:, :, :], q_sb[:, :, :]).then_inc(o_hi_ok, 1)
            act.copy(o_ca_hi[:, :, :], q_ca[:, :, :]).then_inc(o_hi_ok, 1)

            for j in range(N_PROJ, N_PROJ + N_MERGE):
                split_job(j + 1)
                n_gate = (j - N_PROJ) // 2
                if (j - N_PROJ) % 2 == 0:
                    act.wait_ge(chunk_used, job_chunks(j + 1))
                    g, ca = n_gate // 2, n_gate % 2
                    if n_gate >= 1:
                        act.wait_ge(y_taken, n_gate)
                    if n_gate == 2:
                        act.wait_ge(mix_ok, 1)
                    for b in range(4):
                        col = ca * KT + g * 4 + b
                        ins = act.activation(gates[:, b, :], ps[:, b, :], ACT.Sigmoid,
                                             bias=bg_col[:, col:col + 1])
                    ins.then_inc(gate_taken, 1)
                if j == N_PROJ + 6:
                    act.wait_ge(mix_ok, 1)
                    act.copy(hT_hi[:, 0:4, :], mix[:, 0:4, :]).then_inc(mix_hi_ok, 1)
            act.wait_ge(mix_ok, 2)
            act.copy(hT_hi[:, 4:8, :], mix[:, 4:8, :]).then_inc(mix_hi_ok, 1)
            split_job(N_PROJ + N_MERGE + 1)

            def split_expert(i, q):
                act.wait_ge(raw_full[raw_slot(q)], raw_use(i, q))
                if isinstance(i, int) and i == 0 and q < NSPL:
                    act.wait_ge(chunk_used, used_up_to(0, q - NSPL))
                elif isinstance(i, int) and i == 0 and q < ESPL:
                    act.wait_ge(table_ok, 1)
                else:
                    act.wait_ge(chunk_used, used_up_to(i, q - ESPL))
                act.copy(his[spl_slot(q)], raws[raw_slot(q)]).then_inc(hi_ready, 1)

            split_expert(0, 0)
            split_expert(0, 1)

            act.wait_ge(chunk_used, N_SPL1)
            for t in range(NT):
                act.wait_ge(squares, NT + t)
                act.activation(junk2[:, :].rearrange("p (h n) -> p h n", h=2), mixed(t), ACT.Square,
                               accum_out=small[:, 20 + t:21 + t]).then_inc(squares, 1)
            act.wait_ge(mean_sq, 2)
            act.activation(small[:, 28:32], small[:, 24:28], ACT.Sqrt).then_inc(rooted, 1)
            for t in range(NT):
                act.wait_ge(x1_ok, t + 1)
                act.wait_ge(squares, 2 * NT + t)
                act.activation(junk2[:, :], x1[:, t, :], ACT.Square,
                               accum_out=small[:, 40 + t:41 + t]).then_inc(squares, 1)
            act.wait_ge(mean_sq, 3)
            act.activation(small[:, 48:52], small[:, 44:48], ACT.Sqrt).then_inc(rooted, 1)
            split_expert(0, 2)
            for t in range(NT):
                act.wait_ge(h2_turned, t + 1)
                act.copy(h2T[:, :, t * P:(t + 1) * P],
                         psf[:, (t % 2) * 1024:(t % 2) * 1024 + 1024].rearrange("p (k n) -> p k n", k=KT)
                         ).then_inc(h2T_ok, 1)
            act.wait_ge(top_ok, 1)
            act.activation(r_w[:, :, :], logit[:, :, :], ACT.Exp).then_inc(top_exp, 1)

            def x_hi(b):
                act.wait_ge(x_turned, b + 1)
                act.copy(xT_hi[:, :, :], ps[:, 6:8, :].rearrange("p b (k n) -> p (b k) n", n=P)).then_inc(xT_hi_ok, 1)

            def hidden_hi(b):
                act.wait_ge(hid_turned, b + 1)
                act.copy(hidT_hi[:, :, :], ps[:, 6:8, :].rearrange("p b (k n) -> p (b k) n", n=P)).then_inc(hidT_hi_ok, 1)

            def sigmoid(b):
                act.wait_ge(gate_ok, b + 1)
                act.activation(sig[:, :], gate_c[:, :], ACT.Sigmoid, scale=SIG_ALPHA).then_inc(sg_ok, 1)

            def rows_out(b, used):
                act.wait_ge(chunk_used, used)
                if not isinstance(b, int) or b >= 1:
                    act.wait_ge(y_stored, b * 16)
                act.copy(y_out[:, :].rearrange("p (h n) -> p h n", h=2), ps[:, 4:6, :]).then_inc(y_ok, 1)
                act.wait_ge(y_ok, b + 1)
                dst = ys_d[b * SLOTS:(b + 1) * SLOTS, :] if isinstance(b, int) else ys_d[bass.ds(b * SLOTS, SLOTS), :]
                act.dma_start(dst, y_out[:, :]).then_inc(y_stored, 16)

            act.wait_ge(table_ok, 1)
            act.wait_ge(ys_filled, 16 * ((MAXB - E) * SLOTS // S))
            n_mid = act.value_load(expert_of[0:1, MAXB:MAXB + 1], min_val=E - 2, max_val=MAXB - 3)
            nblk = n_mid + 2
            x_hi(0)
            for c_ in range(NSPL, W1C):
                split_expert(0, c_)
            act.wait_ge(chunk_used, used_up_to(0, W1C - 1))
            x_hi(1)
            sigmoid(0)

            def step_of(i, first):
                split_expert(i, 0 - W2C)
                split_expert(i, 1 - W2C)
                hidden_hi(i - 1)
                if not first:
                    rows_out(i - 2, used_up_to(i, -W2C - 1))
                for k in range(2, 11):
                    split_expert(i, k - W2C)
                act.wait_ge(chunk_used, used_up_to(i, W1C - 1 - W2C))
                x_hi(i + 1)
                sigmoid(i)
                split_expert(i, 11 - W2C)

            step_of(1, True)
            step_of(2, False)
            with act.Fori(3, nblk) as i:
                step_of(i, False)
            hidden_hi(n_mid + 1)
            rows_out(n_mid, used_up_to(nblk, -W2C - 1))
            for k in range(W2C):
                split_expert(nblk, k - W2C)
            rows_out(n_mid + 1, used_up_to(nblk, -1))

            for t in range(NT):
                act.wait_ge(ff_ok, t + 1)
                act.wait_ge(squares, 3 * NT + t)
                act.activation(ff_junk[:, :], ff[:, t, :], ACT.Square,
                               accum_out=small[:, 60 + t:61 + t]).then_inc(squares, 1)
                act.wait_ge(mean_sq, 4 + t)
                act.activation(small[:, 68 + t:69 + t], small[:, 64 + t:65 + t], ACT.Sqrt).then_inc(rooted, 1)

        @block.vector
        def _(dve):
            n_step = [0]

            def step(ins):
                n_step[0] += 1
                ins.then_inc(dve_step, 1)
                dve.wait_ge(dve_step, n_step[0])

            def split_lo(n, m, raw_slot, spl_slot):
                dve.wait_ge(hi_ready, m + 1)
                if m >= NSPL:
                    dve.wait_ge(chunk_used, m - NSPL + 1)
                dve.tensor_tensor(w_lo[:, spl_slot, :], raw[:, raw_slot, :], w_hi[:, spl_slot, :].bitcast(F32),
                                  ALU.subtract).then_inc(chunk_read, 1)

            def sum_ada(n, q, k):
                dve.wait_ge(raw_full[n % NRAW], 16 * (n // NRAW + 1))
                if k > 0:
                    dve.wait_ge(chunk_read, n if q == 0 else last_ada[0] + 1)
                dve.scalar_tensor_tensor(out=mod_acc[:, q, :], in0=raw[:, n % NRAW, :], scalar=c_col[:, k:k + 1],
                                         in1=mod_acc[:, q, :], op0=ALU.mult, op1=ALU.add).then_inc(chunk_read, 1)
                last_ada[0] = n

            last_ada = [0]
            place = [0]

            def stream_to(j):
                while place[0] < len(STREAM):
                    n = place[0]
                    item = STREAM[n]
                    if item[0] == "w":
                        if item[1] > j:
                            return
                        m = job_chunks(item[1]) + item[2]
                        split_lo(n, m, n % NRAW, m % NSPL)
                    else:
                        sum_ada(n, item[1], item[2])
                    place[0] += 1

            def root(ms0, n, which):
                ms = small[:, ms0:ms0 + n]
                rt = small[:, ms0 + 4:ms0 + 4 + n]
                y = small[:, ms0 + 8:ms0 + 8 + n]
                t = small[:, ms0 + 12:ms0 + 12 + n]
                dve.wait_ge(rooted, which)
                step(dve.reciprocal(y, rt))
                step(dve.tensor_tensor(t, y, y, ALU.mult))
                step(dve.tensor_tensor(t, t, ms, ALU.mult))
                step(dve.tensor_scalar(t, t, -0.5, 1.5, ALU.mult, ALU.add))
                step(dve.tensor_tensor(y, y, t, ALU.mult))

            dve.memset(mod_acc[:, :, :], 0.0).then_inc(mod_zero, 1)
            dve.wait_ge(squares, NT)
            dve.tensor_scalar(small[:, 4:8], small[:, 0:4], 1.0 / D, EPS, ALU.mult, ALU.add).then_inc(mean_sq, 1)
            dve.wait_ge(bias_hi_ok, 1)
            dve.tensor_tensor(bias_lo[:, :], bias_in[:, :], bias_hi[:, :].bitcast(F32),
                              ALU.subtract).then_inc(bias_lo_ok, 1)
            root(4, NT, 1)
            for t in range(NT):
                ins = dve.tensor_scalar(x_in[:, t, :], x_in[:, t, :], small[:, 12 + t:13 + t], None, ALU.mult)
            step(ins)
            dve.wait_ge(small_in, 32)
            dve.wait_ge(b_row_in, 16)
            stream_to(-1)
            dve.wait_ge(mod_out, 1)
            dve.wait_ge(g1_in, 16)
            dve.tensor_copy(shift1[:, :], psf[:, 4 * 512:4 * 512 + D])
            step(dve.scalar_tensor_tensor(out=scale1[:, :], in0=psf[:, 4 * 512 + D:4 * 512 + 2 * D], scalar=1.0,
                                          in1=junk[:, :], op0=ALU.add, op1=ALU.mult))
            for t in range(NT):
                if t >= 2:
                    dve.wait_ge(h_turned, t - 1)
                step(dve.tensor_tensor(h_rows[:, t % 2, :], x_in[:, t, :], scale1[:, :], ALU.mult))
                dve.tensor_tensor(h_rows[:, t % 2, :], h_rows[:, t % 2, :], shift1[:, :], ALU.add).then_inc(h_ready, 1)
                if t >= 1:
                    turned_lo(dve, t - 1)
            turned_lo(dve, NT - 1)
            stream_to(0)
            for j in range(N_PROJ):
                stream_to(j + 1)

            for h in range(HEADS):
                dve.wait_ge(zc_ok, h + 1)
                dve.wait_ge(rel_masked, h + 1)
                if h >= 1:
                    dve.wait_ge(p_turned, h)
                for i in range(NT):
                    a, n = QOFF[i], QWID[i]
                    ins = dve.tensor_tensor_reduce(zb[:, a:a + n], psf[:, 1536 + a:1536 + a + n],
                                                   rel[:, h % 2, S - n:S], 1.0, NEG, ALU.add, ALU.max,
                                                   small[:, 80 + i:81 + i])
                ins.then_inc(rel_used, 1)
                dve.wait_ge(rel_used, h + 1)
                dve.tensor_scalar(small[:, 84:88], small[:, 80:84], -1.0, None, ALU.mult).then_inc(zb_ok, 1)
                dve.wait_ge(soft_ok, h + 1)
                if h >= 1:
                    dve.wait_ge(sp_lo_ok, h)
                dve.scalar_tensor_tensor(out=sp[:, :], in0=psf[:, 0:SC], scalar=0.0, in1=soft[:, :],
                                         op0=ALU.max, op1=ALU.add).then_inc(sp_ok, 1)
                dve.wait_ge(sp_hi_ok, h + 1)
                dve.tensor_tensor(sp_lo[:, :], sp[:, :], sp_hi[:, :].bitcast(F32), ALU.subtract).then_inc(sp_lo_ok, 1)
                dve.wait_ge(exp_ok, h + 1)
                step(dve.reciprocal(small[:, 92:96], small[:, 88:92]))
                for i in range(NT):
                    zq = zb[:, QOFF[i]:QOFF[i] + QWID[i]]
                    ins = dve.tensor_scalar(zq, zq, small[:, 92 + i:93 + i], None, ALU.mult)
                ins.then_inc(p_ok, 1)
            dve.wait_ge(o_hi_ok, 1)
            dve.tensor_tensor(o_sb_lo[:, :, :], q_sb[:, :, :], o_sb_hi[:, :, :].bitcast(F32), ALU.subtract
                              ).then_inc(o_lo_ok, 1)
            dve.wait_ge(o_hi_ok, 2)
            dve.tensor_tensor(o_ca_lo[:, :, :], q_ca[:, :, :], o_ca_hi[:, :, :].bitcast(F32), ALU.subtract
                              ).then_inc(o_lo_ok, 1)

            for j in range(N_PROJ, N_PROJ + N_MERGE):
                stream_to(j + 1)
                if (j - N_PROJ) % 2 == 0:
                    continue
                n_y = (j - N_PROJ) // 2
                g, ca = n_y // 2, n_y % 2
                dve.wait_ge(gate_taken, n_y + 1)
                dve.wait_ge(chunk_used, job_chunks(j + 1))
                src = ps[:, 4:8, :]
                if not ca:
                    dve.tensor_tensor(mix[:, 4 * g:4 * g + 4, :], src, gates[:, :, :], ALU.mult).then_inc(y_taken, 1)
                else:
                    dve.tensor_tensor(gates[:, :, :], src, gates[:, :, :], ALU.mult).then_inc(y_taken, 1)
                    dve.wait_ge(y_taken, n_y + 1)
                    dve.tensor_tensor(mix[:, 4 * g:4 * g + 4, :], mix[:, 4 * g:4 * g + 4, :], gates[:, :, :],
                                      ALU.add).then_inc(mix_ok, 1)
                if n_y == 2:
                    dve.wait_ge(mix_hi_ok, 1)
                    dve.tensor_tensor(hT_lo[:, 0:4, :], mix[:, 0:4, :], hT_hi[:, 0:4, :].bitcast(F32),
                                      ALU.subtract).then_inc(mix_lo_ok, 1)
            dve.wait_ge(mix_hi_ok, 2)
            dve.tensor_tensor(hT_lo[:, 4:8, :], mix[:, 4:8, :], hT_hi[:, 4:8, :].bitcast(F32),
                              ALU.subtract).then_inc(mix_lo_ok, 1)
            stream_to(len(JOBS))

            def lo_expert(i, q):
                dve.wait_ge(hi_ready, used_up_to(i, q))
                if isinstance(i, int) and i == 0 and q < NSPL:
                    dve.wait_ge(chunk_used, used_up_to(0, q - NSPL))
                elif not (isinstance(i, int) and i == 0 and q < ESPL):
                    dve.wait_ge(chunk_used, used_up_to(i, q - ESPL))
                dve.tensor_tensor(los[spl_slot(q)], raws[raw_slot(q)], his[spl_slot(q)].bitcast(F32),
                                  ALU.subtract).then_inc(chunk_read, 1)

            lo_expert(0, 0)
            lo_expert(0, 1)
            dve.wait_ge(post_in, 16 * 5)
            dve.tensor_tensor(gate_post[:, :], gate_post[:, :], g_row[:, 0, :], ALU.mult)
            step(dve.scalar_tensor_tensor(out=scale2[:, :], in0=scale2[:, :], scalar=1.0, in1=g_row[:, 1, :],
                                          op0=ALU.add, op1=ALU.mult))
            dve.wait_ge(squares, 2 * NT)
            dve.tensor_scalar(small[:, 24:28], small[:, 20:24], 1.0 / D, EPS, ALU.mult, ALU.add).then_inc(mean_sq, 1)
            root(24, NT, 2)
            dve.wait_ge(x_again, 16 * NT)
            for t in range(NT):
                step(dve.scalar_tensor_tensor(out=post[:, :].rearrange("p (h n) -> p h n", h=2), in0=mixed(t),
                                              scalar=small[:, 32 + t:33 + t],
                                              in1=gate_post[:, :].rearrange("p (h n) -> p h n", h=2),
                                              op0=ALU.mult, op1=ALU.mult))
                dve.tensor_tensor(x1[:, t, :], x1[:, t, :], post[:, :], ALU.add).then_inc(x1_ok, 1)
                dve.wait_ge(x1_ok, t + 1)
            dve.wait_ge(squares, 3 * NT)
            dve.tensor_scalar(small[:, 44:48], small[:, 40:44], 1.0 / D, EPS, ALU.mult, ALU.add).then_inc(mean_sq, 1)
            root(44, NT, 3)
            for t in range(NT):
                step(dve.scalar_tensor_tensor(out=post[:, :], in0=x1[:, t, :], scalar=small[:, 52 + t:53 + t],
                                              in1=scale2[:, :], op0=ALU.mult, op1=ALU.mult))
                dve.tensor_tensor(h2[:, t, :], post[:, :], shift2[:, :], ALU.add).then_inc(h2_ok, 1)
                dve.wait_ge(h2_ok, t + 1)
            lo_expert(0, 2)

            dve.wait_ge(logits_ok, 1)
            dve.wait_ge(consts, 9)
            step(dve.tensor_copy(logit[:, :, :], ps[:, 4, 0:NT * E].rearrange("p (t e) -> p t e", t=NT)))
            for t in range(NT):
                ins = dve.max(out=top8[:, t, :], in_=logit[:, t, :])
            step(ins)
            shape = [P, NT, E]
            fourth = top8[:, :, 3:4].to_broadcast(shape)
            dve.tensor_tensor(r_gt[:, :, :], logit[:, :, :], fourth, ALU.is_gt)
            step(dve.tensor_tensor(r_eq[:, :, :], logit[:, :, :], fourth, ALU.is_equal))
            dve.tensor_tensor(logit[:, :, :], logit[:, :, :], top8[:, :, 0:1].to_broadcast(shape),
                              ALU.subtract).then_inc(top_ok, 1)
            step(dve.tensor_reduce(r_sum[:, :, 0:1], r_gt[:, :, :], AX.X, ALU.add))
            step(dve.tensor_scalar(r_sum[:, :, 0:1], r_sum[:, :, 0:1], -1.0, float(TOPK), ALU.mult, ALU.add))
            for t in range(NT):
                ins = dve.tensor_tensor_scan(r_ceq[:, t, :], ones[:, 0:E], r_eq[:, t, :], 0.0, ALU.mult, ALU.add)
            step(ins)
            step(dve.tensor_tensor(r_ceq[:, :, :], r_ceq[:, :, :], r_sum[:, :, 0:1].to_broadcast(shape), ALU.is_le))
            step(dve.tensor_tensor(r_eq[:, :, :], r_eq[:, :, :], r_ceq[:, :, :], ALU.mult))
            dve.tensor_tensor(r_mask[:, :, :], r_gt[:, :, :], r_eq[:, :, :], ALU.add).then_inc(mask_ok, 1)
            dve.wait_ge(mask_ok, 1)
            for t in range(NT):
                ins = dve.tensor_tensor_scan(r_pos[:, t, :], ones[:, 0:E], r_mask[:, t, :], 0.0, ALU.mult, ALU.add)
            step(ins)
            dve.wait_ge(top_exp, 1)
            step(dve.tensor_tensor(r_w[:, :, :], r_w[:, :, :], r_mask[:, :, :], ALU.mult))
            step(dve.tensor_reduce(r_sum[:, :, 1:2], r_w[:, :, :], AX.X, ALU.add))
            step(dve.reciprocal(r_sum[:, :, 2:3], r_sum[:, :, 1:2]))
            step(dve.tensor_tensor(r_w[:, :, :], r_w[:, :, :], r_sum[:, :, 2:3].to_broadcast(shape), ALU.mult))
            dve.wait_ge(rank_ok, 1)
            cnt = ps[:, 6, 0:E]
            step(dve.tensor_scalar(over[:, 0, :], cnt, float(SLOTS), None, ALU.is_gt))
            for q in (2, 3):
                step(dve.scalar_tensor_tensor(out=over[:, 0, :], in0=cnt, scalar=float(q * SLOTS),
                                              in1=over[:, 0, :], op0=ALU.is_gt, op1=ALU.add))
            step(dve.tensor_tensor_scan(over[:, 1, :], ones[:, 0:E], over[:, 0, :], 0.0, ALU.mult, ALU.add))
            step(dve.tensor_tensor(over[:, 2, :], over[:, 1, :], over[:, 0, :], ALU.subtract))
            step(dve.scalar_tensor_tensor(out=over[:, 2, :], in0=over[:, 2, :], scalar=float(E - 1),
                                          in1=iota_e[:, :], op0=ALU.add, op1=ALU.subtract))
            step(dve.tensor_copy(r_rank[:, :, :], ps[:, 5, 0:NT * E].rearrange("p (t e) -> p t e", t=NT)))
            step(dve.tensor_scalar(r_t1[:, :, :], r_rank[:, :, :], float(SLOTS), None, ALU.is_ge))
            step(dve.scalar_tensor_tensor(out=r_t2[:, :, :], in0=r_rank[:, :, :], scalar=float(2 * SLOTS),
                                          in1=r_t1[:, :, :], op0=ALU.is_ge, op1=ALU.add))
            step(dve.scalar_tensor_tensor(out=r_t2[:, :, :], in0=r_rank[:, :, :], scalar=float(3 * SLOTS),
                                          in1=r_t2[:, :, :], op0=ALU.is_ge, op1=ALU.add))
            step(dve.scalar_tensor_tensor(out=r_slot[:, :, :], in0=r_t2[:, :, :], scalar=-float(SLOTS),
                                          in1=r_rank[:, :, :], op0=ALU.mult, op1=ALU.add))
            for t in range(NT):
                ins = dve.tensor_tensor(r_blk[:, t, :], r_t1[:, t, :], over[:, 2, :], ALU.mult)
            step(ins)
            step(dve.tensor_tensor(r_blk[:, :, :], r_blk[:, :, :], r_t2[:, :, :], ALU.add))
            for t in range(NT):
                ins = dve.tensor_tensor(r_blk[:, t, :], r_blk[:, t, :], iota_e[:, :], ALU.add)
            step(ins)
            for k in range(TOPK):
                step(dve.scalar_tensor_tensor(out=r_t1[:, :, :], in0=r_pos[:, :, :], scalar=float(k + 1),
                                              in1=r_mask[:, :, :], op0=ALU.is_equal, op1=ALU.mult))
                for src, dst in ((r_blk, blk4), (r_slot, slot4), (r_w, w4)):
                    step(dve.tensor_tensor(r_t2[:, :, :], r_t1[:, :, :], src[:, :, :], ALU.mult))
                    step(dve.tensor_reduce(dst[:, :, k:k + 1], r_t2[:, :, :], AX.X, ALU.add))
            step(dve.scalar_tensor_tensor(out=d4f[:, :, :], in0=blk4[:, :, :], scalar=float(SLOTS),
                                          in1=slot4[:, :, :], op0=ALU.mult, op1=ALU.add))
            step(dve.tensor_copy(dest4[:, :, :], d4f[:, :, :]))
            n_ov = MAXB - E
            step(dve.tensor_tensor(ov_m[0:1, :, :], over[0:1, 1:2, :].to_broadcast([1, n_ov, E]),
                                   iota_n[0:1, 0:n_ov].rearrange("p (m o) -> p m o", o=1).to_broadcast([1, n_ov, E]),
                                   ALU.is_le))
            dve.tensor_copy(exp_f[0:1, 0:E], iota_e[0:1, :])
            dve.tensor_scalar(exp_f[0:1, MAXB:MAXB + 1], over[0:1, 1, E - 1:E], float(E - 2), None, ALU.add)
            step(dve.tensor_reduce(exp_f[0:1, E:MAXB].rearrange("p (m o) -> p m o", o=1), ov_m[0:1, :, :],
                                   AX.X, ALU.add))
            step(dve.tensor_scalar(exp_f[0:1, E:MAXB], exp_f[0:1, E:MAXB], float(E - 1), None, ALU.min))
            step(dve.tensor_copy(expert_of[0:1, :], exp_f[0:1, :]))
            for n in range(NT * TOPK):
                t, k = n // TOPK, n % TOPK
                if n >= 2:
                    dve.wait_ge(hot_used, n - 1)
                dve.tensor_scalar(hot_r[:, n % 2, :], iota_r[:, :], slot4[:, t, k:k + 1], None, ALU.is_equal)
                dve.tensor_scalar(hot_n[:, n % 2, :], iota_n[:, :], blk4[:, t, k:k + 1], tok_id[:, t:t + 1],
                                  ALU.is_equal, ALU.mult).then_inc(hot_ok, 1)
            dve.wait_ge(hot_used, NT * TOPK)
            dve.tensor_copy(slot_tok[:, :], ps[:, 7, 0:MAXB]).then_inc(table_ok, 1)
            dve.wait_ge(table_ok, 1)

            def x_lo(b):
                dve.wait_ge(xT_hi_ok, b + 1)
                dve.tensor_tensor(xT_lo[:, :, :], ps[:, 6:8, :].rearrange("p b (k n) -> p (b k) n", n=P),
                                  xT_hi[:, :, :].bitcast(F32), ALU.subtract).then_inc(xT_lo_ok, 1)

            def hidden_lo(b):
                dve.wait_ge(hidT_hi_ok, b + 1)
                dve.tensor_tensor(hidT_lo[:, :, :], ps[:, 6:8, :].rearrange("p b (k n) -> p (b k) n", n=P),
                                  hidT_hi[:, :, :].bitcast(F32), ALU.subtract).then_inc(hidT_lo_ok, 1)

            def clamps(b):
                dve.tensor_scalar(gate_c[:, :], psf[:, 0:D], LIMIT, None, ALU.min).then_inc(gate_ok, 1)
                dve.tensor_scalar(up_c[:, :], psf[:, D:2 * D], LIMIT, -LIMIT, ALU.min, ALU.max).then_inc(up_ok, 1)

            def products(b):
                dve.wait_ge(up_ok, b + 1)
                dve.scalar_tensor_tensor(out=up_c[:, :], in0=up_c[:, :], scalar=1.0, in1=gate_c[:, :],
                                         op0=ALU.add, op1=ALU.mult).then_inc(ug_ok, 1)
                dve.wait_ge(ug_ok, b + 1)
                dve.wait_ge(sg_ok, b + 1)
                if not isinstance(b, int) or b >= 1:
                    dve.wait_ge(hid_turned, b)
                dve.tensor_tensor(hid[:, :], up_c[:, :], sig[:, :], ALU.mult).then_inc(hid_ok, 1)

            n_mid = dve.value_load(expert_of[0:1, MAXB:MAXB + 1], min_val=E - 2, max_val=MAXB - 3)
            nblk = n_mid + 2
            x_lo(0)
            for c_ in range(NSPL, W1C):
                lo_expert(0, c_)
            dve.wait_ge(chunk_used, used_up_to(0, W1C - 1))
            x_lo(1)
            clamps(0)
            products(0)

            def step_of(i):
                lo_expert(i, 0 - W2C)
                lo_expert(i, 1 - W2C)
                hidden_lo(i - 1)
                for k in range(2, 11):
                    lo_expert(i, k - W2C)
                dve.wait_ge(chunk_used, used_up_to(i, W1C - 1 - W2C))
                x_lo(i + 1)
                clamps(i)
                lo_expert(i, 11 - W2C)
                products(i)

            with dve.Fori(1, nblk) as i:
                step_of(i)
            hidden_lo(n_mid + 1)
            for k in range(W2C):
                lo_expert(nblk, k - W2C)

            dve.wait_ge(end_in, 32)
            step(dve.tensor_tensor(gate_end[:, :], gate_end[:, :], g_end[:, :], ALU.mult))
            def finish(t):
                dve.wait_ge(squares, 3 * NT + t + 1)
                dve.tensor_scalar(small[:, 64 + t:65 + t], small[:, 60 + t:61 + t], 1.0 / D, EPS, ALU.mult,
                                  ALU.add).then_inc(mean_sq, 1)
                root(64 + t, 1, 4 + t)
                dve.scalar_tensor_tensor(out=o_rows[:, t, :], in0=ff[:, t, :], scalar=small[:, 72 + t:73 + t],
                                         in1=gate_end[:, :], op0=ALU.mult, op1=ALU.mult).then_inc(normed, 1)

            for t in range(NT):
                dve.wait_ge(g_in[t], 16 * TOPK)
                step(dve.tensor_scalar(ff[:, t, :], g_buf[:, t * TOPK, :], w4[:, t, 0:1], None, ALU.mult))
                for k in range(1, TOPK):
                    ins = dve.scalar_tensor_tensor(out=ff[:, t, :], in0=g_buf[:, t * TOPK + k, :],
                                                   scalar=w4[:, t, k:k + 1], in1=ff[:, t, :],
                                                   op0=ALU.mult, op1=ALU.add)
                    if k < TOPK - 1:
                        step(ins)
                ins.then_inc(ff_ok, 1)
                if t >= 1:
                    finish(t - 1)
            finish(NT - 1)

        @block.tensor
        def _(pe):
            mm = pe.matmul

            def three(out_, a_hi, a_lo, b_hi, b_lo, start, stop):
                mm(out_, a_hi, b_hi, start=start, stop=False, skip_group_check=True)
                mm(out_, a_hi, b_lo, start=False, stop=False, skip_group_check=True)
                return mm(out_, a_lo, b_hi, start=False, stop=stop, skip_group_check=True)

            pe.wait_ge(consts, 5)
            pe.wait_ge(chunk_read, KT)
            for n in range(4):
                ins = mm(ps[:, 4 + n, :], ones[:, :], mod_acc[:, 0, n * 512:(n + 1) * 512], start=True, stop=True)
            ins.then_inc(mod_out, 1)
            for t in range(NT):
                pe.wait_ge(h_ready, t + 1)
                if t >= 2:
                    pe.wait_ge(hT_lo_ok, t - 1)
                for k in range(KT):
                    o = (t % 2) * 1024 + k * P
                    ins = pe.transpose(psf[:, o:o + P], h_rows[:, t % 2, k * P:(k + 1) * P], ident[:, :])
                ins.then_inc(h_turned, 1)

            def job(j):
                name, _, _, kt, turned = JOBS[j]
                act_hi, act_lo = {"y_sb": (o_sb_hi, o_sb_lo), "y_ca": (o_ca_hi, o_ca_lo)}.get(name, (hT_hi, hT_lo))
                for c_ in range(kt // 4):
                    m = job_chunks(j) + c_
                    pe.wait_ge(hi_ready, m + 1)
                    n_raw = [n for n, s in enumerate(STREAM) if s == ("w", j, c_)][0]
                    pe.wait_ge(chunk_read, n_raw + 1)
                    wh = w_hi[:, m % NSPL, :].rearrange("p (k n) -> p k n", k=4)
                    wl = w_lo[:, m % NSPL, :].rearrange("p (k n) -> p k n", k=4)
                    for b in range(4):
                        out_ = ps[:, 4 * (j % 2) + b, :]
                        cols = slice(b * P, (b + 1) * P)
                        for k4 in range(4):
                            k = c_ * 4 + k4
                            first, last_ = k == 0, k == kt - 1
                            if turned:
                                ins = three(out_, wh[:, k4, cols], wl[:, k4, cols], act_hi[:, k, :],
                                            act_lo[:, k, :], first, last_)
                            else:
                                ins = three(out_, act_hi[:, k, cols], act_lo[:, k, cols], wh[:, k4, :],
                                            wl[:, k4, :], first, last_)
                    ins.then_inc(chunk_used, 1)

            pe.wait_ge(hT_lo_ok, NT)
            for j in range(N_PROJ):
                if j >= 2:
                    pe.wait_ge(proj_taken, j - 1)
                job(j)
            for q in (1, 2):
                pe.wait_ge(proj_taken, N_PROJ - 2 + q)
                pe.wait_ge(chunk_read, N_ADA_END)
                for n in range(4):
                    ins = mm(ps[0:1, 4 * (q - 1) + n, :], ones[:, 0:1], mod_acc[:, q, n * 512:(n + 1) * 512],
                             start=True, stop=True)
                ins.then_inc(mod_out, 1)

            pe.wait_ge(mod_taken, 2)
            pe.wait_ge(const_r, 3)
            for h in range(HEADS):
                r, p = slice(DH * (h % 2), DH * (h % 2) + DH), h // 2
                if h >= 1:
                    pe.wait_ge(a_ok, h)
                for i in range(NT):
                    a, n = SOFF[i], SWID[i]
                    mm(psf[:, a:a + n], k_sb[r, p, i * P:(i + 1) * P], q_sb[r, p, i * P:S],
                       start=i < 3, stop=False, skip_group_check=True)
                    ins = mm(psf[:, a:a + P], ident_b[:, :], mask_b[:, :], start=False, stop=False,
                             skip_group_check=True)
                ins.then_inc(zs_ok, 1)
                if h >= 1:
                    pe.wait_ge(pT_ok, h)
                for i in (3, 2, 1, 0):
                    a, n = 1536 + QOFF[i], QWID[i]
                    ins = mm(psf[:, a:a + n], q_ca[r, p, i * P:(i + 1) * P], k_ca[r, p, 0:n],
                             start=i > 0, stop=True, skip_group_check=True)
                ins.then_inc(zc_ok, 1)
                pe.wait_ge(sp_hi_ok, h + 1)
                pe.wait_ge(sp_lo_ok, h + 1)
                for i in range(NT):
                    for j in range(i, NT):
                        o = SOFF[i] + P * (j - i)
                        for part in (sp_hi, sp_lo):
                            ins = mm(psf[:, o:o + SWID[j]], neg_tri[:, :] if j == i else neg_ones[:, :],
                                     part[:, SOFF[j]:SOFF[j] + SWID[j]], start=False,
                                     stop=(part is sp_lo and j == NT - 1), skip_group_check=True)
                ins.then_inc(stick_ok, 1)
                pe.wait_ge(p_ok, h + 1)
                for j in range(NT):
                    for i in range(j, NT):
                        o = 1536 + SOFF[j] + P * (i - j)
                        q = QOFF[i] + j * P
                        ins = pe.transpose(psf[:, o:o + P], zb[:, q:q + P], ident[:, :])
                ins.then_inc(p_turned, 1)
                for ok, buf, v, bank, taken, done in ((a_ok, stick, v_sb, 6, os_taken, os_ok),
                                                      (pT_ok, pT, v_ca, 7, oc_taken, oc_ok)):
                    pe.wait_ge(ok, h + 1)
                    if h >= 1:
                        pe.wait_ge(taken, h)
                    for i in range(NT):
                        ins = mm(ps[r, bank, i * P:S], v[:, i, h * DH:(h + 1) * DH],
                                 buf[:, SOFF[i]:SOFF[i] + SWID[i]], start=i == 0, stop=i == NT - 1,
                                 skip_group_check=True)
                    ins.then_inc(done, 1)

            pe.wait_ge(os_taken, HEADS)
            pe.wait_ge(oc_taken, HEADS)
            for j in range(N_PROJ, N_PROJ + N_MERGE):
                n_job = (j - N_PROJ) // 2
                if n_job >= 1:
                    pe.wait_ge(gate_taken if (j - N_PROJ) % 2 == 0 else y_taken, n_job)
                if j == N_PROJ + 1:
                    pe.wait_ge(o_lo_ok, 2)
                job(j)
            pe.wait_ge(mix_lo_ok, 2)
            pe.wait_ge(gate_taken, N_MERGE // 2)
            job(N_PROJ + N_MERGE)
            pe.wait_ge(y_taken, N_MERGE // 2)
            job(N_PROJ + N_MERGE + 1)

            for t in range(NT):
                pe.wait_ge(h2_ok, t + 1)
                if t >= 2:
                    pe.wait_ge(h2T_ok, t - 1)
                for k in range(KT):
                    o = (t % 2) * 1024 + k * P
                    ins = pe.transpose(psf[:, o:o + P], h2[:, t, k * P:(k + 1) * P], ident[:, :])
                ins.then_inc(h2_turned, 1)
            pe.wait_ge(router_in, 32)
            for t in range(NT):
                pe.wait_ge(h2T_ok, t + 1)
                mm(ps[:, 4, t * E:(t + 1) * E], ones[0:1, :], br[0:1, :], start=True, stop=False)
                for k in range(KT):
                    ins = mm(ps[:, 4, t * E:(t + 1) * E], h2T[:, k, t * P:(t + 1) * P], wr[:, k, :],
                             start=False, stop=k == KT - 1)
            ins.then_inc(logits_ok, 1)
            pe.wait_ge(mask_ok, 1)
            for t in range(NT):
                mm(ps[:, 5, t * E:(t + 1) * E], tri[:, :], r_mask[:, t, :], start=True, stop=t == 0)
                for u in range(t):
                    mm(ps[:, 5, t * E:(t + 1) * E], ones[:, :], r_mask[:, u, :], start=False, stop=u == t - 1)
            for t in range(NT):
                ins = mm(ps[:, 6, 0:E], ones[:, :], r_mask[:, t, :], start=t == 0, stop=t == NT - 1)
            ins.then_inc(rank_ok, 1)
            for n in range(NT * TOPK):
                pe.wait_ge(hot_ok, n + 1)
                mm(ps[:, 7, 0:MAXB], hot_r[:, n % 2, :], hot_n[:, n % 2, :], start=n == 0,
                   stop=n == NT * TOPK - 1).then_inc(hot_used, 1)

            def turn(src):
                for k in range(KT):
                    ins = pe.transpose(ps[:, 6 + k // 4, (k % 4) * P:(k % 4 + 1) * P], src[:, k * P:(k + 1) * P],
                                       ident[:, :])
                return ins

            def w_chunk(i, q, bank0, banks, a_hi, a_lo, ktiles, width, last_):
                pe.wait_ge(hi_ready, used_up_to(i, q))
                pe.wait_ge(chunk_read, read_up_to(i, q))
                hi, lo = his[spl_slot(q)], los[spl_slot(q)]
                for n, k in enumerate(ktiles):
                    for a, w in ((a_hi, hi), (a_hi, lo), (a_lo, hi)):
                        for b in range(banks):
                            o = n * width + b * 512
                            ins = mm(ps[:, bank0 + b, :], a[:, k, :], w[:, o:o + 512], start=False,
                                     stop=last_ and k == ktiles[-1] and a is a_lo, skip_group_check=True)
                ins.then_inc(chunk_used, 1)

            def w1_run(b):
                w1_start(b)
                for c_ in range(W1C):
                    w_chunk(b, c_ if isinstance(b, int) and b == 0 else c_ - W2C, 0, 4, xT_hi, xT_lo, (c_,), 0,
                            c_ == W1C - 1)

            def w1_start(b):
                pe.wait_ge(b1_in, b * 16 + 16)
                pe.wait_ge(xT_lo_ok, b + 1)
                if not isinstance(b, int) or b >= 1:
                    pe.wait_ge(up_ok, b)
                for n in range(4):
                    ins = mm(ps[:, n, :], ones_r[:, :], brow1[:, n * 512:(n + 1) * 512], start=True, stop=False,
                             skip_group_check=True)
                ins.then_inc(b1_used, 1)

            def w2_start(b):
                pe.wait_ge(b2_in, b * 16 + 16)
                pe.wait_ge(hidT_lo_ok, b + 1)
                if not isinstance(b, int) or b >= 1:
                    pe.wait_ge(y_ok, b)
                for n in range(2):
                    ins = mm(ps[:, 4 + n, :], ones_r[:, :], brow2[:, n * 512:(n + 1) * 512], start=True, stop=False,
                             skip_group_check=True)
                ins.then_inc(b2_used, 1)

            def w2_run(b, i, q0):
                w2_start(b)
                for c_ in range(W2C):
                    w_chunk(i, q0 + c_, 4, 2, hidT_hi, hidT_lo, (2 * c_, 2 * c_ + 1), D, c_ == W2C - 1)

            def turn_x(b):
                pe.wait_ge(x_gathered, b * 16 + 16)
                if not isinstance(b, int) or b >= 2:
                    pe.wait_ge(hidT_lo_ok, b - 1)
                elif b == 1:
                    pe.wait_ge(xT_lo_ok, 1)
                turn(x_rows).then_inc(x_turned, 1)

            def turn_hidden(b):
                pe.wait_ge(hid_ok, b + 1)
                pe.wait_ge(xT_lo_ok, b + 2)
                turn(hid).then_inc(hid_turned, 1)

            pe.wait_ge(table_ok, 1)
            n_mid = pe.value_load(expert_of[0:1, MAXB:MAXB + 1], min_val=E - 2, max_val=MAXB - 3)
            nblk = n_mid + 2
            turn_x(0)
            w1_run(0)
            turn_x(1)
            turn_hidden(0)

            def step_of(i):
                w1_run(i)
                turn_x(i + 1)
                w2_run(i - 1, i, W1C - W2C)
                turn_hidden(i)

            step_of(1)
            with pe.Fori(2, nblk) as i:
                step_of(i)
            w2_run(n_mid + 1, nblk, -W2C)


_INS = ["x", "c", "w_ada", "b_ada", "g_pre_mix", "g_post_mix", "w_in", "rel_bias", "w_branch_sb", "w_branch_ca",
        "w_gate", "b_gate", "w_out", "g_pre_ffn", "g_post_ffn", "w_router", "b_router", "w_e1", "b_e1", "w_e2",
        "b_e2"]


def kernel(**inputs):
    import numpy as np
    import concourse.bacc as bacc
    from concourse.bass_utils import run_bass_kernel_spmd

    nc = bacc.Bacc("TRN2", target_bir_lowering=False, num_devices=1)
    arrays, args = {}, []
    for name in _INS:
        a = np.asarray(inputs[name])
        if name == "rel_bias":
            at = np.arange(P)[:, None] + (S - P) - np.arange(S)[None, :]
            a = a[0][:, np.clip(at, -REL_CLIP, REL_CLIP) + REL_CLIP]
        a = np.ascontiguousarray(a)
        arrays[f"in_{name}"] = a
        args.append(nc.dram_tensor(f"in_{name}", a.shape, mybir.dt.from_np(a.dtype), kind="ExternalInput").ap())
    args.append(nc.dram_tensor("out_x", (1, S, D), F32, kind="ExternalOutput").ap())
    trunk_layer(nc, *args)
    r = run_bass_kernel_spmd(nc, [arrays], core_ids=[0])
    return r.results[0]["out_x"]
```

```python
from contextlib import ExitStack

import concourse.bass as bass
from concourse import mybir

ALU = mybir.AluOpType
ACT = mybir.ActivationFunctionType
AX = mybir.AxisListType
F32 = mybir.dt.float32
F32R = mybir.dt.float32r
BF16 = mybir.dt.bfloat16
I32 = mybir.dt.int32

P = 128
D = 1024
S = 512
KT = D // P
NT = S // P
HEADS = 8
DH = 64
PAIRS = HEADS // 2
W = HEADS * DH
REL_CLIP = 256
CHUNK = 64
E = 32
TOPK = 4
EPS = 1e-6
SLOTS = P
MAXB = E + (S * TOPK - E) // SLOTS + 1
NEG = -1.0e30
LIMIT = 7.0
SIG_ALPHA = 1.702

CW = 2048
NRAW = 4
NSPL = 3
ERAW = 6
ESPL = 4
BIAS1 = E * 2 * D // P
BIAS = BIAS1 + E * D // P

SOFF = [0, 512, 1024, 896]
SWID = [512, 384, 256, 128]
QOFF = SOFF[::-1]
QWID = SWID[::-1]
SC = 1280

JOBS = [("q_sb", "w_in", 0, KT, True), ("k_sb", "w_in", W, KT, True), ("v_sb", "w_in", 2 * W, KT, False),
        ("q_ca", "w_in", 3 * W, KT, True), ("k_ca", "w_in", 4 * W, KT, True), ("v_ca", "w_in", 5 * W, KT, False)]
JOBS += [("gate_sb", "w_gate", 0, KT, True), ("gate_sb", "w_gate", 512, KT, True),
         ("gate_ca", "w_gate", D, KT, True), ("y_sb", "w_branch_sb", 0, NT, True),
         ("y_sb", "w_branch_sb", 512, NT, True), ("y_ca", "w_branch_ca", 0, NT, True),
         ("gate_ca", "w_gate", D + 512, KT, True), ("y_ca", "w_branch_ca", 512, NT, True)]
JOBS += [("out", "w_out", 0, KT, False), ("out", "w_out", 512, KT, False)]
N_PROJ = 6
N_MERGE = 8
N_BESIDE = 2

STREAM = [("ada", 0, k) for k in range(KT)]
_later = [("ada", q, k) for q in (1, 2) for k in range(KT)]
for _j, (_n, _w, _c, _kt, _t) in enumerate(JOBS):
    STREAM += [("w", _j, c) for c in range(_kt // 4)]
    if _j < N_PROJ:
        _take = 3 if _j < 4 else 2
        STREAM += _later[:_take]
        _later = _later[_take:]
N_RAW1 = len(STREAM)
N_SPL1 = sum(1 for s in STREAM if s[0] == "w")
assert N_RAW1 % NRAW == 0 and not _later
W1C = D * 2 * D // (P * CW)
W2C = D * D // (P * CW)
EC = W1C + W2C
N_ADA_END = max(n for n, s in enumerate(STREAM) if s[0] == "ada") + 1
assert EC % ERAW == 0 and EC % ESPL == 0
SPL_ORDER = [(N_SPL1 + i) % NSPL for i in range(NSPL)] + list(range(NSPL, ESPL))


def raw_slot(q):
    return q % ERAW


def spl_slot(q):
    return SPL_ORDER[q % ESPL]


def raw_use(i, q):
    before = N_RAW1 // NRAW if raw_slot(q) < NRAW else 0
    return i * (16 * EC // ERAW) + 16 * (before + q // ERAW + 1)


def read_up_to(i, q):
    return i * EC + (N_RAW1 + q + 1)


def used_up_to(i, q):
    return i * EC + (N_SPL1 + q + 1)


def job_chunks(j):
    return sum(job[3] // 4 for job in JOBS[:j])


def raw_chunks(j):
    return [(n, s) for n, s in enumerate(STREAM) if s[0] == "w" and s[1] == j]


def row_ap(t, offset, n, parts=P):
    return bass.AP(t.tensor, offset, [[0, parts], [1, n]])


def trunk_layer(nc, x, c, w_ada, b_ada, g_pre_mix, g_post_mix, w_in, rel_tiles, w_branch_sb, w_branch_ca,
                w_gate, b_gate, w_out, g_pre_ffn, g_post_ffn, w_router, b_router, w_e1, b_e1, w_e2, b_e2, out):
    ctx = ExitStack()
    with ctx:
        base = [(nc.sbuf_base + 63) // 64 * 64]

        def at(name, shape, dt, offset):
            return nc.alloc_sbuf_tensor_at(name, shape, dt, offset=offset)

        def bytes_of(shape):
            n = 4
            for s in shape[1:]:
                n *= s
            return (n + 63) // 64 * 64

        def keep(name, shape, dt=F32):
            t = at(name, shape, dt, base[0])
            base[0] += bytes_of(shape)
            return t

        raw = keep("raw", [P, NRAW, CW])
        w_hi = keep("w_hi", [P, NSPL, CW], F32R)
        w_lo = keep("w_lo", [P, NSPL, CW], F32R)
        ident = keep("ident", [P, P])
        ident_b = keep("ident_b", [P, P], BF16)
        mask_b = keep("mask_b", [P, P], BF16)
        ones = keep("ones", [P, P])
        neg_tri = keep("neg_tri", [P, P], F32R)
        neg_ones = keep("neg_ones", [P, P], F32R)
        g_col = keep("g_col", [P, KT])
        mod1_col = keep("mod1_col", [P, 2 * KT])
        mod_col = keep("mod_col", [P, 4 * KT])
        mod_row = keep("mod_row", [4 * KT, P])
        c_col = keep("c_col", [P, KT])
        bg_col = keep("bg_col", [P, 2 * KT])
        small = keep("small", [P, 96])

        arena = base[0]
        limit = 229344

        class Region:

            def __init__(self, start):
                self.pos = start

            def __call__(self, name, shape, dt=F32):
                t = at(name, shape, dt, self.pos)
                self.pos += bytes_of(shape)
                assert self.pos <= limit, (name, self.pos)
                return t

        B = Region(arena)
        hT_hi = B("hT_hi", [P, KT, S], F32R)
        hT_lo = B("hT_lo", [P, KT, S], F32R)
        c0 = B.pos
        C = Region(c0)
        q_sb = C("q_sb", [P, PAIRS, S])
        k_sb = C("k_sb", [P, PAIRS, S])
        v_sb = C("v_sb", [P, NT, W])
        q_ca = C("q_ca", [P, PAIRS, S])
        k_ca = C("k_ca", [P, PAIRS, S])
        v_ca = C("v_ca", [P, NT, W])
        d0 = C.pos
        A = Region(c0)
        x_in = A("x_in", [P, NT, D])
        xT = A("xT", [P, KT, S])
        junk = A("junk", [P, D])
        bias_in = A("bias_in", [P, BIAS])
        bias_hi = A("bias_hi", [P, BIAS], F32R)
        bias_lo = A("bias_lo", [P, BIAS], F32R)
        assert A.pos <= d0
        Dm = Region(d0)
        mod_acc = Dm("mod_acc", [P, 3, CW])
        tri_f = Dm("tri_f", [P, P])
        Da = Region(d0)
        soft = Da("soft", [P, SC])
        sp_lo = at("sp_lo", [P, SC], F32R, Da.pos)
        sp = Da("sp", [P, SC])
        sp_hi = Da("sp_hi", [P, SC], F32R)
        stick = Da("stick", [P, SC])
        pT = at("pT", [P, SC], F32, Da.pos)
        zb = Da("zb", [P, SC])
        rel = Da("rel", [P, S])
        gates_sb = at("gates_sb", [P, KT, S], F32, limit - KT * S * 4)
        assert Da.pos <= limit - KT * S * 4
        o_sb_hi = at("o_sb_hi", [P, PAIRS, S], F32R, c0 + 8 * 1024)
        o_sb_lo = at("o_sb_lo", [P, PAIRS, S], F32R, c0 + 16 * 1024)
        o_ca_hi = at("o_ca_hi", [P, PAIRS, S], F32R, c0 + 32 * 1024)
        o_ca_lo = at("o_ca_lo", [P, PAIRS, S], F32R, c0 + 40 * 1024)
        Dg = Region(d0)
        gates = Dg("gates", [P, 4, S])
        mix = Dg("mix", [P, KT, S])
        assert Dg.pos <= limit - KT * S * 4
        Z = Region(c0)
        x1 = Z("x1", [P, NT, D])
        F = Region(Z.pos)
        gate_post = F("gate_post", [P, D])
        scale2 = F("scale2", [P, D])
        shift2 = F("shift2", [P, D])
        g_row = F("g_row", [P, 2, D])
        h2 = F("h2", [P, NT, D])
        post = F("post", [P, D])
        junk2 = F("junk2", [P, D])
        h2T = at("h2T", [P, KT, S], F32, arena)
        hot_r = at("hot_r", [P, NT * TOPK, P], F32, F.pos - 8 * D)
        hot_n = at("hot_n", [P, NT * TOPK, MAXB], F32, arena)
        R = Region(arena + 16 * 1024)
        logit_t = R("logit_t", [E, S])
        logit = R("logit", [P, NT, E])
        top8 = R("top8", [P, NT, 8])
        r_gt = R("r_gt", [P, NT, E])
        r_eq = R("r_eq", [P, NT, E])
        r_ceq = R("r_ceq", [P, NT, E])
        r_mask = R("r_mask", [P, NT, E], BF16)
        r_pos = R("r_pos", [P, NT, E])
        r_w = R("r_w", [P, NT, E])
        r_dest = R("r_dest", [P, NT, E])
        r_sum = R("r_sum", [P, NT, E])
        r_sel = R("r_sel", [P, TOPK, NT * E])
        r_val = R("r_val", [P, TOPK, NT * E])
        over = R("over", [P, 4, E])
        slot4 = R("slot4", [P, TOPK, NT])
        blk4 = R("blk4", [P, TOPK, NT])
        blk4_i = R("blk4_i", [P, TOPK, NT], I32)
        d4f = R("d4f", [P, TOPK, NT])
        ov_m = R("ov_m", [1, MAXB - E, E])
        exp_f = R("exp_f", [1, MAXB + 1])
        assert R.pos <= c0
        K = Region(F.pos + (ERAW - NRAW) * CW * 4 + 2 * D * 4)
        wr = K("wr", [P, KT, E])
        br = K("br", [1, E])
        iota_e = K("iota_e", [P, E])
        iota_r = K("iota_r", [P, P])
        iota_n = K("iota_n", [P, MAXB])
        iota_k = K("iota_k", [P, TOPK])
        tok_id = K("tok_id", [P, NT])
        ones_r = K("ones_r", [2, P], F32R)
        tri = K("tri", [P, P], BF16)
        ones_b = K("ones_b", [P, P], BF16)
        w4 = K("w4", [P, TOPK, NT])
        dest4 = K("dest4", [P, TOPK, NT], I32)
        slot_tok = K("slot_tok", [P, MAXB], I32)
        idx_now = K("idx_now", [P, 1], I32)
        expert_of = K("expert_of", [1, MAXB + 1], I32)
        raw_more = at("raw_more", [P, ERAW - NRAW, CW], F32, F.pos)
        hi_more = at("hi_more", [P, ESPL - NSPL, CW], F32R, arena + 8192)
        lo_more = at("lo_more", [P, ESPL - NSPL, CW], F32R, arena + 16384)
        assert arena + 24576 <= c0 and ESPL == NSPL + 1
        raws = [raw[:, i, :] for i in range(NRAW)] + [raw_more[:, i, :] for i in range(ERAW - NRAW)]
        his = [w_hi[:, i, :] for i in range(NSPL)] + [hi_more[:, i, :] for i in range(ESPL - NSPL)]
        los = [w_lo[:, i, :] for i in range(NSPL)] + [lo_more[:, i, :] for i in range(ESPL - NSPL)]
        M = Region(Z.pos)
        x_rows = M("x_rows", [P, D])
        xT_hi = M("xT_hi", [P, KT, P], F32R)
        xT_lo = M("xT_lo", [P, KT, P], F32R)
        gate_c = M("gate_c", [P, D])
        up_c = M("up_c", [P, D])
        sig = M("sig", [P, D])
        hid = M("hid", [P, D])
        y_out = M("y_out", [P, D])
        hidT_hi = at("hidT_hi", [P, KT, P], F32R, arena)
        hidT_lo = at("hidT_lo", [P, KT, P], F32R, arena + 4096)
        brow1 = M("brow1", [2, 2 * D], F32R)
        brow2 = M("brow2", [2, D], F32R)
        assert M.pos <= F.pos
        gate_end = at("gate_end", [P, D], F32, F.pos + (ERAW - NRAW) * CW * 4)
        g_end = at("g_end", [P, D], F32, F.pos + (ERAW - NRAW) * CW * 4 + 4096)
        ring0 = (nc.sbuf_base + 63) // 64 * 64
        g_buf = at("g_buf", [P, NT * TOPK, D], F32, ring0)
        T = Region(Z.pos)
        ff = T("ff", [P, NT, D])
        ff_junk = T("ff_junk", [P, D])
        o_rows = T("o_rows", [P, NT, D])
        assert NT * TOPK * D * 4 <= (NRAW + 2 * NSPL) * CW * 4

        ps = ctx.enter_context(nc.psum_tensor("ps", [P, 8, 512], F32))
        psf = ps[:, :, :].rearrange("p b n -> p (b n)")

        mod_d = nc.dram_tensor("mod_rows", (1, 6 * D), F32, kind="Internal").ap()
        bias1_d = nc.dram_tensor("bias1_parts", (2, E, 2 * D), F32, kind="Internal").ap()
        bias2_d = nc.dram_tensor("bias2_parts", (2, E, D), F32, kind="Internal").ap()
        h2_d = nc.dram_tensor("h2_rows", (S, D), F32, kind="Internal").ap()
        ys_d = nc.dram_tensor("expert_rows", (MAXB * SLOTS, D), F32, kind="Internal").ap()

        def sem(name):
            return ctx.enter_context(nc.semaphore(name))

        raw_full = [sem(f"raw_full{i}") for i in range(ERAW)]
        chunk_read = sem("chunk_read")
        hi_ready = sem("hi_ready")
        lo_ready = sem("lo_ready")
        chunk_used = sem("chunk_used")
        small_in = sem("small_in")
        x_loaded = [sem(f"x_loaded{t}") for t in range(NT)]
        b_row1_in = sem("b_row1_in")
        bias_loaded = sem("bias_loaded")
        b_row_in = sem("b_row_in")
        consts = sem("consts")
        pool_step = sem("pool_step")
        passed = sem("passed")
        const_r = sem("const_r")
        dve_step = sem("dve_step")
        act_step = sem("act_step")
        mod_zero = sem("mod_zero")
        mod_summed = sem("mod_summed")
        mod_out = sem("mod_out")
        mod_turned = sem("mod_turned")
        mod_taken = sem("mod_taken")
        mod_stored = sem("mod_stored")
        squares = sem("squares")
        mean_sq = sem("mean_sq")
        rooted = sem("rooted")
        out_done = sem("out_done")
        post_sq = sem("post_sq")
        post_mean = sem("post_mean")
        post_root = sem("post_root")
        x1_sq = sem("x1_sq")
        x1_mean = sem("x1_mean")
        x1_root = sem("x1_root")
        rs_ok = sem("rs_ok")
        xn_ok = sem("xn_ok")
        xn_turned = sem("xn_turned")
        xT_ok = sem("xT_ok")
        h_ready = sem("h_ready")
        hT_hi_ok = sem("hT_hi_ok")
        hT_lo_ok = sem("hT_lo_ok")
        bias_hi_ok = sem("bias_hi_ok")
        bias_lo_ok = sem("bias_lo_ok")
        bias_stored = sem("bias_stored")
        proj_taken = sem("proj_taken")
        gate_taken = sem("gate_taken")
        y_taken = sem("y_taken")
        mix_ok = sem("mix_ok")
        o_hi_ok = sem("o_hi_ok")
        o_lo_ok = sem("o_lo_ok")
        mix_hi_ok = sem("mix_hi_ok")
        mix_lo_ok = sem("mix_lo_ok")
        rel_in = sem("rel_in")
        pre_ok = sem("pre_ok")
        pre_taken = sem("pre_taken")
        gates_sb_ok = sem("gates_sb_ok")
        rel_used = sem("rel_used")
        rel_masked = sem("rel_masked")
        zs_ok = sem("zs_ok")
        zc_ok = sem("zc_ok")
        soft_ok = sem("soft_ok")
        sp_ok = sem("sp_ok")
        sp_hi_ok = sem("sp_hi_ok")
        sp_lo_ok = sem("sp_lo_ok")
        stick_ok = sem("stick_ok")
        a_ok = sem("a_ok")
        zb_ok = sem("zb_ok")
        exp_ok = sem("exp_ok")
        p_ok = sem("p_ok")
        p_turned = sem("p_turned")
        pT_ok = sem("pT_ok")
        os_ok = sem("os_ok")
        oc_ok = sem("oc_ok")
        os_taken = sem("os_taken")
        oc_taken = sem("oc_taken")
        post_in = sem("post_in")
        x_again = sem("x_again")
        x1_ok = sem("x1_ok")
        h2_ok = sem("h2_ok")
        h2_stored = sem("h2_stored")
        h2_turned = sem("h2_turned")
        h2T_ok = sem("h2T_ok")
        router_in = sem("router_in")
        logits_ok = sem("logits_ok")
        logit_t_ok = sem("logit_t_ok")
        logits_back = sem("logits_back")
        top_ok = sem("top_ok")
        top_exp = sem("top_exp")
        mask_ok = sem("mask_ok")
        rank_ok = sem("rank_ok")
        hot_ok = sem("hot_ok")
        hot_used = sem("hot_used")
        table_ok = sem("table_ok")
        idx_ok = sem("idx_ok")
        x_gathered = sem("x_gathered")
        x_turned = sem("x_turned")
        xT_hi_ok = sem("xT_hi_ok")
        xT_lo_ok = sem("xT_lo_ok")
        b1_in = sem("b1_in")
        b1_used = sem("b1_used")
        b2_in = sem("b2_in")
        b2_used = sem("b2_used")
        gate_ok = sem("gate_ok")
        up_ok = sem("up_ok")
        sg_ok = sem("sg_ok")
        ug_ok = sem("ug_ok")
        hid_ok = sem("hid_ok")
        hid_turned = sem("hid_turned")
        hidT_hi_ok = sem("hidT_hi_ok")
        hidT_lo_ok = sem("hidT_lo_ok")
        y_ok = sem("y_ok")
        y_stored = sem("y_stored")
        g_in = [sem(f"g_in{t}") for t in range(NT)]
        ys_filled = sem("ys_filled")
        end_in = sem("end_in")
        ff_ok = sem("ff_ok")
        normed = sem("normed")
        out_ok = sem("out_ok")
        out_stored = sem("out_stored")

        block = ctx.enter_context(nc.Block())

        weights = {"w_in": w_in[0], "w_gate": w_gate[0], "w_branch_sb": w_branch_sb[0],
                   "w_branch_ca": w_branch_ca[0], "w_out": w_out[0]}

        def mixed(t):
            return ps[:, 2 * t:2 * t + 2, :]

        def out_bank(j, b):
            half = j - N_PROJ - N_MERGE
            return 4 * (j % 2) + b if half < 0 else 2 * b + half

        @block.sync
        def _(sp_):
            sp_.dma_start(c_col[:, :], c[0].rearrange("(k p) -> p k", p=P),
                          allow_slow_non_contiguous=True).then_inc(small_in, 16)
            sp_.dma_start(bg_col[:, :], b_gate[0].rearrange("(k p) -> p k", p=P),
                          allow_slow_non_contiguous=True).then_inc(small_in, 16)
            sp_.dma_start(g_col[:, :], g_pre_mix[0].rearrange("(k p) -> p k", p=P),
                          allow_slow_non_contiguous=True).then_inc(small_in, 16)
            for n, item in enumerate(STREAM):
                if n >= NRAW:
                    sp_.wait_ge(chunk_read, n - NRAW + 1)
                slot = raw[:, n % NRAW, :]
                if item[0] == "ada":
                    _, q, k = item
                    src = w_ada[0, k * P:(k + 1) * P, q * CW:(q + 1) * CW]
                else:
                    _, j, half = item
                    _, wname, col, _, _ = JOBS[j]
                    src = weights[wname][half * 512:(half + 1) * 512, col:col + 512].rearrange(
                        "(k p) n -> p k n", p=P)
                    slot = slot.rearrange("p (k n) -> p k n", k=4)
                sp_.dma_start(slot, src).then_inc(raw_full[n % NRAW], 16)

            def load(i, q, src, k):
                slot = raw_slot(q)
                if isinstance(i, int) and NRAW <= q < ERAW:
                    sp_.wait_ge(chunk_used, job_chunks(N_PROJ + N_MERGE))
                    sp_.wait_ge(mix_lo_ok, 2)
                else:
                    sp_.wait_ge(chunk_read, read_up_to(i, q - (NRAW if isinstance(i, int) and q < NRAW else ERAW)))
                dst = raws[slot] if k == 1 else raws[slot].rearrange("p (k n) -> p k n", k=k)
                sp_.dma_start(dst, src).then_inc(raw_full[slot], 16)

            def w1_rows(e, c_):
                return w_e1[0, bass.ds(e, 1), c_ * P:(c_ + 1) * P, :].rearrange("e p n -> p (e n)")

            def w2_rows(e, c_):
                return w_e2[0, bass.ds(e, 1), c_ * 2 * P:(c_ + 1) * 2 * P, :].rearrange("e (k p) n -> p (e k) n", p=P)

            for c_ in range(W1C):
                load(0, c_, w_e1[0, 0, c_ * P:(c_ + 1) * P, :], 1)
            sp_.wait_ge(table_ok, 1)
            n_mid = sp_.value_load(expert_of[0:1, MAXB:MAXB + 1], min_val=E - 2, max_val=MAXB - 3)
            nblk = n_mid + 2
            with sp_.Fori(1, nblk) as i:
                e_now = sp_.value_load(expert_of[0:1, bass.ds(i, 1)], min_val=0, max_val=E - 1)
                for c_ in range(W1C):
                    load(i, c_ - W2C, w1_rows(e_now, c_), 1)
                e_was = sp_.value_load(expert_of[0:1, bass.ds(i - 1, 1)], min_val=0, max_val=E - 1)
                for c_ in range(W2C):
                    load(i, c_ + W1C - W2C, w2_rows(e_was, c_), 2)
            e_last = sp_.value_load(expert_of[0:1, bass.ds(n_mid + 1, 1)], min_val=0, max_val=E - 1)
            for c_ in range(W2C):
                load(nblk, c_ - W2C, w2_rows(e_last, c_), 2)

        @block.gpsimd
        def _(pool):
            n_step = [0]

            def step(ins):
                n_step[0] += 1
                ins.then_inc(pool_step, 1)
                pool.wait_ge(pool_step, n_step[0])

            xr = x[0].rearrange("(t p) d -> p t d", p=P)
            for t in range(NT):
                pool.dma_start(x_in[:, t, :], xr[:, t, :]).then_inc(x_loaded[t], 16)
            step(pool.memset(ones[:, :], 1.0))
            step(pool.memset(tri_f[:, :], 0.0))
            pool.affine_select(out=ident[:, :], in_=tri_f[:, :], compare_op=ALU.not_equal, fill=1.0, base=0,
                               pattern=[[-1, P]], channel_multiplier=1).then_inc(consts, 1)
            pool.affine_select(out=ident_b[:, :], in_=tri_f[:, :], compare_op=ALU.not_equal, fill=1.0, base=0,
                               pattern=[[-1, P]], channel_multiplier=1).then_inc(consts, 1)
            pool.affine_select(out=mask_b[:, :], in_=tri_f[:, :], compare_op=ALU.is_gt, fill=NEG, base=0,
                               pattern=[[1, P]], channel_multiplier=-1).then_inc(consts, 1)
            pool.wait_ge(consts, 3)
            pool.affine_select(out=tri_f[:, :], in_=tri_f[:, :], compare_op=ALU.is_gt, fill=-1.0, base=0,
                               pattern=[[1, P]], channel_multiplier=-1).then_inc(consts, 1)

            step(pool.memset(mod_acc[:, 1:3, :], 0.0))
            pool.dma_start(mod_acc[0:1, 1:3, :], b_ada[0:1, CW:3 * CW].rearrange("o (q n) -> o q n", n=CW)
                           ).then_inc(b_row_in, 16)
            pool.wait_ge(chunk_read, KT)
            pool.dma_start(bias_in[:, 0:BIAS1], b_e1[0].rearrange("e (a n) -> (e a) n", n=BIAS1)
                           ).then_inc(bias_loaded, 16)
            pool.dma_start(bias_in[:, BIAS1:BIAS], b_e2[0].rearrange("e (a n) -> (e a) n", n=BIAS - BIAS1)
                           ).then_inc(bias_loaded, 16)
            for part, ok, buf in ((0, bias_hi_ok, bias_hi), (1, bias_lo_ok, bias_lo)):
                pool.wait_ge(ok, 1)
                pool.dma_start(bias1_d[part].rearrange("e (a n) -> (e a) n", n=BIAS1),
                               buf[:, 0:BIAS1].bitcast(F32)).then_inc(bias_stored, 16)
                pool.dma_start(bias2_d[part].rearrange("e (a n) -> (e a) n", n=BIAS - BIAS1),
                               buf[:, BIAS1:BIAS].bitcast(F32)).then_inc(bias_stored, 16)

            def fill_rows():
                for q in range((MAXB - E) * SLOTS // S):
                    pool.dma_start(ys_d[E * SLOTS + q * S:E * SLOTS + (q + 1) * S, :], x[0]).then_inc(ys_filled, 16)

            for h in range(HEADS):
                if h >= 1:
                    pool.wait_ge(rel_used, h)
                pool.dma_start(rel[:, :], rel_tiles[h]).then_inc(rel_in, 16)
                pool.wait_ge(rel_in, 16 * (h + 1))
                pool.memset(rel[0:CHUNK, S - CHUNK:S], NEG).then_inc(rel_masked, 1)
                if h == 1:
                    fill_rows()

            pool.wait_ge(chunk_used, job_chunks(N_PROJ + N_MERGE))
            pool.wait_ge(mod_stored, 16)
            pool.dma_start(gate_post[:, :], row_ap(mod_d, 2 * D, D)).then_inc(post_in, 16)
            pool.dma_start(shift2[:, :], row_ap(mod_d, 3 * D, D)).then_inc(post_in, 16)
            pool.dma_start(scale2[:, :], row_ap(mod_d, 4 * D, D)).then_inc(post_in, 16)
            pool.dma_start(g_row[:, 0, :], row_ap(g_post_mix, 0, D)).then_inc(post_in, 16)
            pool.dma_start(g_row[:, 1, :], row_ap(g_pre_ffn, 0, D)).then_inc(post_in, 16)
            for t in range(NT):
                pool.dma_start(x1[:, t, :], xr[:, t, :]).then_inc(x_again, 16)
            pool.wait_ge(mix_lo_ok, 2)
            pool.dma_start(wr[:, :, :], w_router[0].rearrange("(k p) e -> p k e", p=P)).then_inc(router_in, 16)
            pool.dma_start(br[:, :], b_router[0:1, :]).then_inc(router_in, 16)
            pool.iota(iota_e[:, :], pattern=[[1, E]], base=0, channel_multiplier=0,
                      allow_small_or_imprecise_dtypes=True).then_inc(consts, 1)
            pool.iota(iota_r[:, :], pattern=[[1, P]], base=0, channel_multiplier=0,
                      allow_small_or_imprecise_dtypes=True).then_inc(consts, 1)
            pool.iota(iota_n[:, :], pattern=[[1, MAXB]], base=0, channel_multiplier=0,
                      allow_small_or_imprecise_dtypes=True).then_inc(consts, 1)
            pool.iota(tok_id[:, :], pattern=[[P, NT]], base=0, channel_multiplier=1,
                      allow_small_or_imprecise_dtypes=True).then_inc(consts, 1)
            pool.iota(iota_k[:, :], pattern=[[1, TOPK]], base=1, channel_multiplier=0,
                      allow_small_or_imprecise_dtypes=True).then_inc(consts, 1)
            pool.memset(ones_b[:, :], 1.0).then_inc(consts, 1)
            pool.affine_select(out=tri[:, :], in_=ones[:, :], compare_op=ALU.is_gt, fill=0.0, base=0,
                               pattern=[[1, P]], channel_multiplier=-1).then_inc(consts, 1)
            for t in range(NT):
                pool.wait_ge(h2_ok, t + 1)
                pool.dma_start(h2_d[t * P:(t + 1) * P, :], h2[:, t, :]).then_inc(h2_stored, 16)

            pool.dma_start(gate_end[:, :], row_ap(mod_d, 5 * D, D)).then_inc(end_in, 16)
            pool.dma_start(g_end[:, :], row_ap(g_post_ffn, 0, D)).then_inc(end_in, 16)

            pool.wait_ge(table_ok, 1)
            pool.wait_ge(h2_stored, 16 * NT)
            pool.wait_ge(h2_turned, NT)
            pool.wait_ge(bias_stored, 64)
            n_mid = pool.value_load(expert_of[0:1, MAXB:MAXB + 1], min_val=E - 2, max_val=MAXB - 3)
            nblk = n_mid + 2

            def gather_x(b):
                pool.tensor_copy(idx_now[:, :], slot_tok[:, b:b + 1] if isinstance(b, int)
                                 else slot_tok[:, bass.ds(b, 1)]).then_inc(idx_ok, 1)
                pool.wait_ge(idx_ok, b + 1)
                pool.sem_inc(passed, 1)
                pool.indirect_dma_start(
                    out=x_rows[:, :], out_offset=None, in_=h2_d[:, :],
                    in_offset=bass.IndirectOffsetOnAxis(ap=idx_now[:, 0:1], axis=0)).then_inc(x_gathered, 16)

            def load_b1(e):
                pool.dma_start(brow1[:, :].bitcast(F32).rearrange("q (o n) -> q o n", o=1),
                               bias1_d[:, bass.ds(e, 1), :]).then_inc(b1_in, 16)

            def load_b2(e):
                pool.dma_start(brow2[:, :].bitcast(F32).rearrange("q (o n) -> q o n", o=1),
                               bias2_d[:, bass.ds(e, 1), :]).then_inc(b2_in, 16)

            gather_x(0)
            load_b1(0)
            pool.wait_ge(x_turned, 1)
            gather_x(1)
            pool.wait_ge(b1_used, 1)
            load_b1(1)
            load_b2(0)
            with pool.Fori(1, nblk) as i:
                pool.wait_ge(x_turned, i + 1)
                gather_x(i + 1)
                e_next = pool.value_load(expert_of[0:1, bass.ds(i + 1, 1)], min_val=0, max_val=E - 1)
                pool.wait_ge(b1_used, i + 1)
                load_b1(e_next)
                e_now = pool.value_load(expert_of[0:1, bass.ds(i, 1)], min_val=0, max_val=E - 1)
                pool.wait_ge(b2_used, i)
                load_b2(e_now)

            pool.wait_ge(y_stored, nblk * 16)
            pool.sem_inc(passed, 1)
            for t in range(NT):
                for k in range(TOPK):
                    pool.indirect_dma_start(
                        out=g_buf[:, t * TOPK + k, :], out_offset=None, in_=ys_d[:, :],
                        in_offset=bass.IndirectOffsetOnAxis(ap=dest4[:, k, t:t + 1], axis=0)).then_inc(g_in[t], 16)
            orow = out[0].rearrange("(t p) d -> p t d", p=P)
            for t in range(NT):
                pool.wait_ge(normed, t + 1)
                pool.tensor_tensor(o_rows[:, t, :], o_rows[:, t, :], x1[:, t, :], ALU.add).then_inc(out_ok, 1)
                pool.wait_ge(out_ok, t + 1)
                pool.dma_start(orow[:, t, :], o_rows[:, t, :]).then_inc(out_stored, 16)
            pool.wait_ge(out_stored, 16 * NT)

        @block.scalar
        def _(act):
            n_step = [0]

            def step(ins):
                n_step[0] += 1
                ins.then_inc(act_step, 1)
                act.wait_ge(act_step, n_step[0])

            def split_hi(n, m, raw_slot, raw_count, spl_slot):
                act.wait_ge(raw_full[raw_slot], raw_count)
                if not isinstance(m, int) or m >= NSPL:
                    act.wait_ge(chunk_used, m - NSPL + 1)
                act.copy(w_hi[:, spl_slot, :], raw[:, raw_slot, :]).then_inc(hi_ready, 1)

            def split_job(j, chunks=(0, 1)):
                for q, (n, item) in enumerate(raw_chunks(j)):
                    m = job_chunks(j) + q
                    if q in chunks:
                        split_hi(n, m, n % NRAW, 16 * (n // NRAW + 1), m % NSPL)

            act.wait_ge(mod_zero, 1)
            act.dma_start(mod_acc[0:1, 0, :], b_ada[0:1, 0:CW]).then_inc(b_row1_in, 16)
            act.wait_ge(consts, 4)
            act.copy(neg_tri[:, :], tri_f[:, :]).then_inc(const_r, 1)
            act.mul(neg_ones[:, :], ones[:, :], -1.0).then_inc(const_r, 1)

            for t in range(NT):
                act.wait_ge(x_loaded[t], 16)
                if t >= 1:
                    act.wait_ge(squares, t)
                act.activation(junk[:, :], x_in[:, t, :], ACT.Square,
                               accum_out=small[:, t:t + 1]).then_inc(squares, 1)
            act.wait_ge(mean_sq, 1)
            act.activation(small[:, 8:12], small[:, 4:8], ACT.Sqrt).then_inc(rooted, 1)
            act.wait_ge(rs_ok, 1)
            for t in range(NT):
                act.mul(x_in[:, t, :], x_in[:, t, :], small[:, 12 + t:13 + t]).then_inc(xn_ok, 1)
            for t in range(NT):
                act.wait_ge(xn_turned, t + 1)
                act.copy(xT[:, :, t * P:(t + 1) * P],
                         ps[:, 2 * t:2 * t + 2, :].rearrange("p h (k n) -> p (h k) n", n=P)).then_inc(xT_ok, 1)
            split_job(0, (0,))
            for k in range(KT):
                act.wait_ge(h_ready, k + 1)
                act.copy(hT_hi[:, k, :], xT[:, k, :]).then_inc(hT_hi_ok, 1)
            split_job(0, (1,))

            for j in range(N_PROJ):
                split_job(j + 1)
                if j == 0:
                    act.wait_ge(bias_loaded, 32)
                    act.copy(bias_hi[:, :], bias_in[:, :]).then_inc(bias_hi_ok, 1)
                if j == 4:
                    act.wait_ge(bias_stored, 64)
                act.wait_ge(chunk_used, job_chunks(j + 1))
                dst = [q_sb, k_sb, v_sb, q_ca, k_ca, v_ca][j]
                src = ps[:, 4 * (j % 2):4 * (j % 2) + 4, :]
                if j % 3 == 0:
                    act.mul(dst[:, :, :], src, DH ** -0.5).then_inc(proj_taken, 1)
                else:
                    act.copy(dst[:, :, :], src).then_inc(proj_taken, 1)
            act.wait_ge(mod_out, 2)
            act.copy(mod_col[:, :], ps[:, 3, 0:4 * KT]).then_inc(mod_taken, 1)

            def take_outputs(h):
                r, p = DH * (h % 2), h // 2
                act.wait_ge(oc_ok, h + 1)
                act.copy(q_ca[r:r + DH, p, :], ps[DH - r:2 * DH - r, 6, :]).then_inc(oc_taken, 1)
                act.wait_ge(os_ok, h + 1)
                act.copy(q_sb[r:r + DH, p, :], ps[r:r + DH, 6, :]).then_inc(os_taken, 1)

            for h in range(HEADS):
                if h == 2:
                    split_job(N_PROJ + 1, (0,))
                elif h == 4:
                    split_job(N_PROJ + 1, (1,))
                elif h == 5:
                    split_job(N_PROJ + 2, (0,))
                act.wait_ge(zs_ok, h + 1)
                if h >= 1:
                    act.wait_ge(sp_ok, h)
                step(act.activation(soft[:, :], psf[:, 0:SC], ACT.Abs))
                step(act.activation(soft[:, :], soft[:, :], ACT.Exp, scale=-1.0))
                act.activation(soft[:, :], soft[:, :], ACT.Ln, bias=1.0).then_inc(soft_ok, 1)
                if h >= 1:
                    take_outputs(h - 1)
                else:
                    act.wait_ge(mod_turned, 1)
                    act.copy(mod_row[:, :], ps[0:4 * KT, 6, 0:P]).then_inc(mod_taken, 1)
                    act.wait_ge(mod_taken, 2)
                    act.dma_start(mod_d[0:1, CW:3 * CW].rearrange("o (n p) -> (o n) p", p=P),
                                  mod_row[:, :]).then_inc(mod_stored, 16)
                act.wait_ge(sp_ok, h + 1)
                if h >= 1:
                    act.wait_ge(stick_ok, h)
                act.copy(sp_hi[:, :], sp[:, :]).then_inc(sp_hi_ok, 1)
                act.wait_ge(zb_ok, h + 1)
                for i in range(NT):
                    zq = zb[:, QOFF[i]:QOFF[i] + QWID[i]]
                    ins = act.activation(zq, zq, ACT.Exp, bias=small[:, 84 + i:85 + i],
                                         accum_out=small[:, 88 + i:89 + i])
                ins.then_inc(exp_ok, 1)
                act.wait_ge(stick_ok, h + 1)
                if h >= 1:
                    act.wait_ge(os_ok, h)
                act.activation(stick[:, :], psf[:, 0:SC], ACT.Exp).then_inc(a_ok, 1)
                act.wait_ge(p_turned, h + 1)
                act.copy(pT[:, :], psf[:, 3 * 512:3 * 512 + SC]).then_inc(pT_ok, 1)
            take_outputs(HEADS - 1)
            split_job(N_PROJ + 2, (1,))
            act.wait_ge(oc_taken, HEADS)
            act.wait_ge(os_taken, HEADS)
            act.copy(o_sb_hi[:, :, :], q_sb[:, :, :]).then_inc(o_hi_ok, 1)
            act.copy(o_ca_hi[:, :, :], q_ca[:, :, :]).then_inc(o_hi_ok, 1)
            act.wait_ge(pre_taken, HEADS)
            act.activation(gates_sb[:, :, :], gates_sb[:, :, :], ACT.Sigmoid).then_inc(gates_sb_ok, 1)

            def gate_ca(j, n_gate):
                act.wait_ge(chunk_used, job_chunks(j + 1))
                if n_gate == 1:
                    act.wait_ge(mix_ok, 1)
                for b in range(4):
                    col = KT + n_gate * 4 + b
                    ins = act.activation(gates[:, b, :], ps[:, b, :], ACT.Sigmoid, bias=bg_col[:, col:col + 1])
                ins.then_inc(gate_taken, 1)

            first = N_PROJ + N_BESIDE
            split_job(first + 1)
            gate_ca(first, 0)
            for j in range(first + 2, first + 6):
                split_job(j)
            gate_ca(first + 4, 1)
            act.copy(hT_hi[:, 0:4, :], mix[:, 0:4, :]).then_inc(mix_hi_ok, 1)
            split_job(N_PROJ + N_MERGE)
            act.wait_ge(mix_ok, 2)
            act.copy(hT_hi[:, 4:8, :], mix[:, 4:8, :]).then_inc(mix_hi_ok, 1)
            split_job(N_PROJ + N_MERGE + 1)

            def split_expert(i, q):
                act.wait_ge(raw_full[raw_slot(q)], raw_use(i, q))
                if isinstance(i, int) and i == 0 and q < NSPL:
                    act.wait_ge(chunk_used, used_up_to(0, q - NSPL))
                elif isinstance(i, int) and i == 0 and q < ESPL:
                    act.wait_ge(table_ok, 1)
                else:
                    act.wait_ge(chunk_used, used_up_to(i, q - ESPL))
                act.copy(his[spl_slot(q)], raws[raw_slot(q)]).then_inc(hi_ready, 1)

            split_expert(0, 0)

            def root_x1(t):
                act.wait_ge(x1_mean, t + 1)
                act.activation(small[:, 48 + t:49 + t], small[:, 44 + t:45 + t], ACT.Sqrt).then_inc(x1_root, 1)

            def copy_h2T(t):
                act.wait_ge(h2_turned, t + 1)
                act.copy(h2T[:, :, t * P:(t + 1) * P],
                         mixed(t).rearrange("p h (k n) -> p (h k) n", n=P)).then_inc(h2T_ok, 1)

            for t in range(NT):
                act.wait_ge(out_done, t + 1)
                if t >= 1:
                    act.wait_ge(x1_sq, t)
                act.activation(junk2[:, :].rearrange("p (h n) -> p h n", h=2), mixed(t), ACT.Square,
                               accum_out=small[:, 20 + t:21 + t]).then_inc(post_sq, 1)
                act.wait_ge(post_mean, t + 1)
                act.activation(small[:, 28 + t:29 + t], small[:, 24 + t:25 + t], ACT.Sqrt).then_inc(post_root, 1)
                if t >= 1:
                    root_x1(t - 1)
                act.wait_ge(x1_ok, t + 1)
                act.wait_ge(post_sq, t + 1)
                act.activation(junk2[:, :], x1[:, t, :], ACT.Square,
                               accum_out=small[:, 40 + t:41 + t]).then_inc(x1_sq, 1)
                if t >= 2:
                    copy_h2T(t - 2)
            root_x1(NT - 1)
            copy_h2T(NT - 2)
            copy_h2T(NT - 1)
            act.wait_ge(logits_ok, 1)
            act.copy(logit_t[:, :], ps[0:E, 0, :]).then_inc(logit_t_ok, 1)
            act.copy(ones_r[:, :], ones[0:2, :]).then_inc(const_r, 1)
            act.wait_ge(top_ok, 1)
            act.activation(r_w[:, :, :], logit[:, :, :], ACT.Exp).then_inc(top_exp, 1)
            split_expert(0, 1)
            split_expert(0, 2)

            def x_hi(b):
                act.wait_ge(x_turned, b + 1)
                act.copy(xT_hi[:, :, :], ps[:, 6:8, :].rearrange("p b (k n) -> p (b k) n", n=P)).then_inc(xT_hi_ok, 1)

            def hidden_hi(b):
                act.wait_ge(hid_turned, b + 1)
                act.copy(hidT_hi[:, :, :], ps[:, 6:8, :].rearrange("p b (k n) -> p (b k) n", n=P)).then_inc(hidT_hi_ok, 1)

            def sigmoid(b):
                act.wait_ge(gate_ok, b + 1)
                act.activation(sig[:, :], gate_c[:, :], ACT.Sigmoid, scale=SIG_ALPHA).then_inc(sg_ok, 1)

            def rows_out(b, used):
                act.wait_ge(chunk_used, used)
                if not isinstance(b, int) or b >= 1:
                    act.wait_ge(y_stored, b * 16)
                act.copy(y_out[:, :].rearrange("p (h n) -> p h n", h=2), ps[:, 4:6, :]).then_inc(y_ok, 1)
                act.wait_ge(y_ok, b + 1)
                dst = ys_d[b * SLOTS:(b + 1) * SLOTS, :] if isinstance(b, int) else ys_d[bass.ds(b * SLOTS, SLOTS), :]
                act.dma_start(dst, y_out[:, :]).then_inc(y_stored, 16)

            act.wait_ge(table_ok, 1)
            act.wait_ge(ys_filled, 16 * ((MAXB - E) * SLOTS // S))
            n_mid = act.value_load(expert_of[0:1, MAXB:MAXB + 1], min_val=E - 2, max_val=MAXB - 3)
            nblk = n_mid + 2
            x_hi(0)
            for c_ in range(NSPL, W1C):
                split_expert(0, c_)
            act.wait_ge(chunk_used, used_up_to(0, W1C - 1))
            x_hi(1)
            sigmoid(0)

            def step_of(i, first):
                split_expert(i, 0 - W2C)
                split_expert(i, 1 - W2C)
                hidden_hi(i - 1)
                if not first:
                    rows_out(i - 2, used_up_to(i, -W2C - 1))
                for k in range(2, 11):
                    split_expert(i, k - W2C)
                act.wait_ge(chunk_used, used_up_to(i, W1C - 1 - W2C))
                x_hi(i + 1)
                sigmoid(i)
                split_expert(i, 11 - W2C)

            step_of(1, True)
            step_of(2, False)
            with act.Fori(3, nblk) as i:
                step_of(i, False)
            hidden_hi(n_mid + 1)
            rows_out(n_mid, used_up_to(nblk, -W2C - 1))
            for k in range(W2C):
                split_expert(nblk, k - W2C)
            rows_out(n_mid + 1, used_up_to(nblk, -1))

            for t in range(NT):
                act.wait_ge(ff_ok, t + 1)
                act.wait_ge(squares, NT + t)
                act.activation(ff_junk[:, :], ff[:, t, :], ACT.Square,
                               accum_out=small[:, 60 + t:61 + t]).then_inc(squares, 1)
                act.wait_ge(mean_sq, 2 + t)
                act.activation(small[:, 68 + t:69 + t], small[:, 64 + t:65 + t], ACT.Sqrt).then_inc(rooted, 1)

        @block.vector
        def _(dve):
            n_step = [0]

            def step(ins):
                n_step[0] += 1
                ins.then_inc(dve_step, 1)
                dve.wait_ge(dve_step, n_step[0])

            def split_lo(n, m, raw_slot, spl_slot):
                dve.wait_ge(hi_ready, m + 1)
                if m >= NSPL:
                    dve.wait_ge(chunk_used, m - NSPL + 1)
                dve.tensor_tensor(w_lo[:, spl_slot, :], raw[:, raw_slot, :], w_hi[:, spl_slot, :].bitcast(F32),
                                  ALU.subtract).then_inc(chunk_read, 1)

            def sum_ada(n, q, k):
                dve.wait_ge(raw_full[n % NRAW], 16 * (n // NRAW + 1))
                if k == 0:
                    dve.wait_ge(b_row1_in if q == 0 else b_row_in, 16)
                if k > 0:
                    dve.wait_ge(chunk_read, n if q == 0 else last_ada[0] + 1)
                dve.scalar_tensor_tensor(out=mod_acc[:, q, :], in0=raw[:, n % NRAW, :], scalar=c_col[:, k:k + 1],
                                         in1=mod_acc[:, q, :], op0=ALU.mult, op1=ALU.add).then_inc(chunk_read, 1)
                last_ada[0] = n

            last_ada = [0]
            place = [0]

            def stream_to(j):
                while place[0] < len(STREAM):
                    n = place[0]
                    item = STREAM[n]
                    if item[0] == "w":
                        if item[1] > j:
                            return
                        m = job_chunks(item[1]) + item[2]
                        split_lo(n, m, n % NRAW, m % NSPL)
                    else:
                        sum_ada(n, item[1], item[2])
                    place[0] += 1

            def stream_one():
                n = place[0]
                m = job_chunks(STREAM[n][1]) + STREAM[n][2]
                split_lo(n, m, n % NRAW, m % NSPL)
                place[0] += 1

            def root(ms0, n, rooted_by, which, done=None):
                ms = small[:, ms0:ms0 + n]
                rt = small[:, ms0 + 4:ms0 + 4 + n]
                y = small[:, ms0 + 8:ms0 + 8 + n]
                t = small[:, ms0 + 12:ms0 + 12 + n]
                dve.wait_ge(rooted_by, which)
                step(dve.reciprocal(y, rt))
                step(dve.tensor_tensor(t, y, y, ALU.mult))
                step(dve.tensor_tensor(t, t, ms, ALU.mult))
                step(dve.tensor_scalar(t, t, -0.5, 1.5, ALU.mult, ALU.add))
                if done is None:
                    step(dve.tensor_tensor(y, y, t, ALU.mult))
                else:
                    dve.tensor_tensor(y, y, t, ALU.mult).then_inc(done, 1)

            dve.memset(mod_acc[:, 0, :], 0.0).then_inc(mod_zero, 1)
            dve.wait_ge(small_in, 48)
            for k in range(KT):
                if k == 4:
                    dve.wait_ge(squares, NT)
                    dve.tensor_scalar(small[:, 4:8], small[:, 0:4], 1.0 / D, EPS, ALU.mult,
                                      ALU.add).then_inc(mean_sq, 1)
                    root(4, NT, rooted, 1, rs_ok)
                sum_ada(k, 0, k)
                place[0] += 1
            stream_one()
            dve.wait_ge(mod_out, 1)
            dve.tensor_copy(mod1_col[:, 0:KT], ps[:, 4, 0:KT])
            step(dve.scalar_tensor_tensor(out=mod1_col[:, KT:2 * KT], in0=ps[:, 4, KT:2 * KT], scalar=1.0,
                                          in1=g_col[:, :], op0=ALU.add, op1=ALU.mult))

            def modulate(k):
                dve.tensor_scalar(xT[:, k, :], xT[:, k, :], mod1_col[:, KT + k:KT + k + 1], mod1_col[:, k:k + 1],
                                  ALU.mult, ALU.add).then_inc(h_ready, 1)

            dve.wait_ge(xT_ok, NT)
            modulate(0)
            modulate(1)
            for k in range(KT):
                if k + 2 < KT:
                    modulate(k + 2)
                dve.wait_ge(hT_hi_ok, k + 1)
                dve.tensor_tensor(hT_lo[:, k, :], xT[:, k, :], hT_hi[:, k, :].bitcast(F32),
                                  ALU.subtract).then_inc(hT_lo_ok, 1)
            stream_to(0)
            for j in range(N_PROJ):
                stream_to(j + 1)
                if j == 0:
                    dve.wait_ge(bias_hi_ok, 1)
                    dve.tensor_tensor(bias_lo[:, :], bias_in[:, :], bias_hi[:, :].bitcast(F32),
                                      ALU.subtract).then_inc(bias_lo_ok, 1)

            for h in range(HEADS):
                if h in (2, 4, 5):
                    stream_one()
                dve.wait_ge(soft_ok, h + 1)
                if h >= 1:
                    dve.wait_ge(stick_ok, h)
                dve.scalar_tensor_tensor(out=sp[:, :], in0=psf[:, 0:SC], scalar=0.0, in1=soft[:, :],
                                         op0=ALU.max, op1=ALU.add).then_inc(sp_ok, 1)
                dve.wait_ge(zc_ok, h + 1)
                dve.wait_ge(rel_masked, h + 1)
                if h >= 1:
                    dve.wait_ge(oc_ok, h)
                for i in range(NT):
                    a, n = QOFF[i], QWID[i]
                    ins = dve.tensor_tensor_reduce(zb[:, a:a + n], psf[:, 1536 + a:1536 + a + n],
                                                   rel[:, S - n:S], 1.0, NEG, ALU.add, ALU.max,
                                                   small[:, 80 + i:81 + i])
                ins.then_inc(rel_used, 1)
                dve.wait_ge(rel_used, h + 1)
                dve.tensor_scalar(small[:, 84:88], small[:, 80:84], -1.0, None, ALU.mult).then_inc(zb_ok, 1)
                dve.wait_ge(sp_hi_ok, h + 1)
                dve.tensor_tensor(sp_lo[:, :], sp[:, :], sp_hi[:, :].bitcast(F32), ALU.subtract).then_inc(sp_lo_ok, 1)
                dve.wait_ge(exp_ok, h + 1)
                step(dve.reciprocal(small[:, 92:96], small[:, 88:92]))
                for i in range(NT):
                    zq = zb[:, QOFF[i]:QOFF[i] + QWID[i]]
                    ins = dve.tensor_scalar(zq, zq, small[:, 92 + i:93 + i], None, ALU.mult)
                ins.then_inc(p_ok, 1)
                dve.wait_ge(pre_ok, h + 1)
                dve.tensor_scalar(gates_sb[:, h, :], ps[:, 7, :], bg_col[:, h:h + 1], None,
                                  ALU.add).then_inc(pre_taken, 1)
            stream_one()
            dve.wait_ge(o_hi_ok, 1)
            dve.tensor_tensor(o_sb_lo[:, :, :], q_sb[:, :, :], o_sb_hi[:, :, :].bitcast(F32), ALU.subtract
                              ).then_inc(o_lo_ok, 1)
            dve.wait_ge(o_hi_ok, 2)
            dve.tensor_tensor(o_ca_lo[:, :, :], q_ca[:, :, :], o_ca_hi[:, :, :].bitcast(F32), ALU.subtract
                              ).then_inc(o_lo_ok, 1)

            first = N_PROJ + N_BESIDE

            def y_times_gate(j, dst, gate):
                stream_to(j + 1)
                dve.wait_ge(chunk_used, job_chunks(j + 1))
                b0 = 4 * (j % 2)
                dve.tensor_tensor(dst, ps[:, b0:b0 + 4, :], gate, ALU.mult).then_inc(y_taken, 1)

            def add_branch(g):
                dve.wait_ge(y_taken, 3 + g)
                half = mix[:, 4 * g:4 * g + 4, :]
                dve.tensor_tensor(half, half, gates[:, :, :], ALU.add).then_inc(mix_ok, 1)

            def mix_lo(g):
                dve.wait_ge(mix_hi_ok, g + 1)
                k = slice(4 * g, 4 * g + 4)
                dve.tensor_tensor(hT_lo[:, k, :], mix[:, k, :], hT_hi[:, k, :].bitcast(F32),
                                  ALU.subtract).then_inc(mix_lo_ok, 1)

            stream_to(first)
            dve.wait_ge(gates_sb_ok, 1)
            y_times_gate(first + 1, mix[:, 0:4, :], gates_sb[:, 0:4, :])
            y_times_gate(first + 2, mix[:, 4:8, :], gates_sb[:, 4:8, :])
            dve.wait_ge(gate_taken, 1)
            y_times_gate(first + 3, gates[:, :, :], gates[:, :, :])
            add_branch(0)
            stream_to(first + 5)
            mix_lo(0)
            dve.wait_ge(gate_taken, 2)
            y_times_gate(first + 5, gates[:, :, :], gates[:, :, :])
            add_branch(1)
            mix_lo(1)
            stream_to(len(JOBS))

            def lo_expert(i, q):
                dve.wait_ge(hi_ready, used_up_to(i, q))
                if isinstance(i, int) and i == 0 and q < NSPL:
                    dve.wait_ge(chunk_used, used_up_to(0, q - NSPL))
                elif not (isinstance(i, int) and i == 0 and q < ESPL):
                    dve.wait_ge(chunk_used, used_up_to(i, q - ESPL))
                dve.tensor_tensor(los[spl_slot(q)], raws[raw_slot(q)], his[spl_slot(q)].bitcast(F32),
                                  ALU.subtract).then_inc(chunk_read, 1)

            dve.wait_ge(post_in, 16 * 5)
            dve.tensor_tensor(gate_post[:, :], gate_post[:, :], g_row[:, 0, :], ALU.mult)
            step(dve.scalar_tensor_tensor(out=scale2[:, :], in0=scale2[:, :], scalar=1.0, in1=g_row[:, 1, :],
                                          op0=ALU.add, op1=ALU.mult))
            dve.wait_ge(x_again, 16 * NT)
            lo_expert(0, 0)

            def mean(ms0, sq0, sq_ok, t, done):
                dve.wait_ge(sq_ok, t + 1)
                dve.tensor_scalar(small[:, ms0 + t:ms0 + t + 1], small[:, sq0 + t:sq0 + t + 1], 1.0 / D, EPS,
                                  ALU.mult, ALU.add).then_inc(done, 1)

            def h2_of(t):
                root(44 + t, 1, x1_root, t + 1)
                step(dve.scalar_tensor_tensor(out=h2[:, t, :], in0=x1[:, t, :], scalar=small[:, 52 + t:53 + t],
                                              in1=scale2[:, :], op0=ALU.mult, op1=ALU.mult))
                dve.tensor_tensor(h2[:, t, :], h2[:, t, :], shift2[:, :], ALU.add).then_inc(h2_ok, 1)

            for t in range(NT):
                mean(24, 20, post_sq, t, post_mean)
                root(24 + t, 1, post_root, t + 1)
                step(dve.scalar_tensor_tensor(out=post[:, :].rearrange("p (h n) -> p h n", h=2), in0=mixed(t),
                                              scalar=small[:, 32 + t:33 + t],
                                              in1=gate_post[:, :].rearrange("p (h n) -> p h n", h=2),
                                              op0=ALU.mult, op1=ALU.mult))
                dve.tensor_tensor(x1[:, t, :], x1[:, t, :], post[:, :], ALU.add).then_inc(x1_ok, 1)
                dve.wait_ge(x1_ok, t + 1)
                if t >= 1:
                    h2_of(t - 1)
                mean(44, 40, x1_sq, t, x1_mean)
            h2_of(NT - 1)

            dve.wait_ge(logits_back, 1)
            dve.wait_ge(consts, 11)
            step(dve.tensor_copy(logit[:, :, :], ps[:, 4, 0:NT * E].rearrange("p (t e) -> p t e", t=NT)))
            for t in range(NT):
                ins = dve.max(out=top8[:, t, :], in_=logit[:, t, :])
            step(ins)
            shape = [P, NT, E]
            fourth = top8[:, :, 3:4].to_broadcast(shape)
            dve.tensor_tensor(r_gt[:, :, :], logit[:, :, :], fourth, ALU.is_gt)
            step(dve.tensor_tensor(r_eq[:, :, :], logit[:, :, :], fourth, ALU.is_equal))
            dve.tensor_tensor(logit[:, :, :], logit[:, :, :], top8[:, :, 0:1].to_broadcast(shape),
                              ALU.subtract).then_inc(top_ok, 1)
            step(dve.tensor_reduce(r_sum[:, :, 0:1], r_gt[:, :, :], AX.X, ALU.add))
            step(dve.tensor_scalar(r_sum[:, :, 0:1], r_sum[:, :, 0:1], -1.0, float(TOPK), ALU.mult, ALU.add))
            for t in range(NT):
                ins = dve.tensor_tensor_scan(r_ceq[:, t, :], ones[:, 0:E], r_eq[:, t, :], 0.0, ALU.mult, ALU.add)
            step(ins)
            step(dve.tensor_tensor(r_ceq[:, :, :], r_ceq[:, :, :], r_sum[:, :, 0:1].to_broadcast(shape), ALU.is_le))
            step(dve.tensor_tensor(r_eq[:, :, :], r_eq[:, :, :], r_ceq[:, :, :], ALU.mult))
            dve.tensor_tensor(r_mask[:, :, :], r_gt[:, :, :], r_eq[:, :, :], ALU.add).then_inc(mask_ok, 1)
            dve.wait_ge(mask_ok, 1)
            for t in range(NT):
                ins = dve.tensor_tensor_scan(r_pos[:, t, :], ones[:, 0:E], r_mask[:, t, :], 0.0, ALU.mult, ALU.add)
            step(ins)
            step(dve.tensor_tensor(r_pos[:, :, :], r_pos[:, :, :], r_mask[:, :, :], ALU.mult))
            wide = [P, TOPK, NT * E]
            step(dve.tensor_tensor(r_sel[:, :, :],
                                   r_pos[:, :, :].rearrange("p (o t) e -> p o (t e)", o=1).to_broadcast(wide),
                                   iota_k[:, :].rearrange("p (k o) -> p k o", o=1).to_broadcast(wide),
                                   ALU.is_equal))

            def choose(src, dst):
                step(dve.tensor_tensor(r_val[:, :, :], r_sel[:, :, :],
                                       src[:, :, :].rearrange("p (o t) e -> p o (t e)", o=1).to_broadcast(wide),
                                       ALU.mult))
                step(dve.tensor_reduce(dst[:, :, :].rearrange("p k (t o) -> p (k t) o", o=1),
                                       r_val[:, :, :].rearrange("p k (t e) -> p (k t) e", e=E), AX.X, ALU.add))

            dve.wait_ge(top_exp, 1)
            step(dve.tensor_tensor(r_w[:, :, :], r_w[:, :, :], r_mask[:, :, :], ALU.mult))
            step(dve.tensor_reduce(r_sum[:, :, 1:2], r_w[:, :, :], AX.X, ALU.add))
            step(dve.reciprocal(r_sum[:, :, 2:3], r_sum[:, :, 1:2]))
            step(dve.tensor_tensor(r_w[:, :, :], r_w[:, :, :], r_sum[:, :, 2:3].to_broadcast(shape), ALU.mult))
            choose(r_w, w4)
            dve.wait_ge(rank_ok, 1)
            cnt = ps[:, 6, 0:E]
            step(dve.tensor_scalar(over[:, 0, :], cnt, float(SLOTS), None, ALU.is_gt))
            for q in (2, 3):
                step(dve.scalar_tensor_tensor(out=over[:, 0, :], in0=cnt, scalar=float(q * SLOTS),
                                              in1=over[:, 0, :], op0=ALU.is_gt, op1=ALU.add))
            step(dve.tensor_tensor_scan(over[:, 1, :], ones[:, 0:E], over[:, 0, :], 0.0, ALU.mult, ALU.add))
            step(dve.tensor_tensor(over[:, 2, :], over[:, 1, :], over[:, 0, :], ALU.subtract))
            step(dve.scalar_tensor_tensor(out=over[:, 2, :], in0=over[:, 2, :], scalar=float(E - 1),
                                          in1=iota_e[:, :], op0=ALU.add, op1=ALU.subtract))
            rank = ps[:, 5, 0:NT * E].rearrange("p (t e) -> p t e", t=NT)
            step(dve.tensor_scalar(r_dest[:, :, :], rank, float(SLOTS), None, ALU.is_ge))
            step(dve.tensor_tensor(r_dest[:, :, :], r_dest[:, :, :], over[:, 2:3, :].to_broadcast(shape), ALU.mult))
            step(dve.tensor_tensor(r_dest[:, :, :], r_dest[:, :, :],
                                   iota_e[:, :].rearrange("p (o e) -> p o e", o=1).to_broadcast(shape), ALU.add))
            step(dve.scalar_tensor_tensor(out=r_dest[:, :, :], in0=r_dest[:, :, :], scalar=float(SLOTS), in1=rank,
                                          op0=ALU.mult, op1=ALU.add))
            choose(r_dest, d4f)
            step(dve.tensor_copy(dest4[:, :, :], d4f[:, :, :]))
            step(dve.tensor_scalar(blk4_i[:, :, :], dest4[:, :, :], SLOTS.bit_length() - 1, None,
                                   ALU.logical_shift_right))
            step(dve.tensor_copy(blk4[:, :, :], blk4_i[:, :, :]))
            step(dve.scalar_tensor_tensor(out=slot4[:, :, :], in0=blk4[:, :, :], scalar=-float(SLOTS),
                                          in1=d4f[:, :, :], op0=ALU.mult, op1=ALU.add))
            for t in range(NT):
                n = slice(t * TOPK, (t + 1) * TOPK)
                w_r, w_n = [P, TOPK, P], [P, TOPK, MAXB]
                dve.tensor_tensor(hot_r[:, n, :], iota_r[:, :].rearrange("p (o n) -> p o n", o=1).to_broadcast(w_r),
                                  slot4[:, :, t:t + 1].to_broadcast(w_r), ALU.is_equal)
                step(dve.tensor_tensor(hot_n[:, n, :],
                                       iota_n[:, :].rearrange("p (o n) -> p o n", o=1).to_broadcast(w_n),
                                       blk4[:, :, t:t + 1].to_broadcast(w_n), ALU.is_equal))
                dve.tensor_scalar(hot_n[:, n, :], hot_n[:, n, :], tok_id[:, t:t + 1], None,
                                  ALU.mult).then_inc(hot_ok, 1)
            n_ov = MAXB - E
            step(dve.tensor_tensor(ov_m[0:1, :, :], over[0:1, 1:2, :].to_broadcast([1, n_ov, E]),
                                   iota_n[0:1, 0:n_ov].rearrange("p (m o) -> p m o", o=1).to_broadcast([1, n_ov, E]),
                                   ALU.is_le))
            dve.tensor_copy(exp_f[0:1, 0:E], iota_e[0:1, :])
            dve.tensor_scalar(exp_f[0:1, MAXB:MAXB + 1], over[0:1, 1, E - 1:E], float(E - 2), None, ALU.add)
            step(dve.tensor_reduce(exp_f[0:1, E:MAXB].rearrange("p (m o) -> p m o", o=1), ov_m[0:1, :, :],
                                   AX.X, ALU.add))
            step(dve.tensor_scalar(exp_f[0:1, E:MAXB], exp_f[0:1, E:MAXB], float(E - 1), None, ALU.min))
            step(dve.tensor_copy(expert_of[0:1, :], exp_f[0:1, :]))
            dve.wait_ge(hot_used, 1)
            dve.tensor_copy(slot_tok[:, :], ps[:, 7, 0:MAXB]).then_inc(table_ok, 1)
            lo_expert(0, 1)
            lo_expert(0, 2)
            dve.wait_ge(table_ok, 1)

            def x_lo(b):
                dve.wait_ge(xT_hi_ok, b + 1)
                dve.tensor_tensor(xT_lo[:, :, :], ps[:, 6:8, :].rearrange("p b (k n) -> p (b k) n", n=P),
                                  xT_hi[:, :, :].bitcast(F32), ALU.subtract).then_inc(xT_lo_ok, 1)

            def hidden_lo(b):
                dve.wait_ge(hidT_hi_ok, b + 1)
                dve.tensor_tensor(hidT_lo[:, :, :], ps[:, 6:8, :].rearrange("p b (k n) -> p (b k) n", n=P),
                                  hidT_hi[:, :, :].bitcast(F32), ALU.subtract).then_inc(hidT_lo_ok, 1)

            def clamps(b):
                dve.tensor_scalar(gate_c[:, :], psf[:, 0:D], LIMIT, None, ALU.min).then_inc(gate_ok, 1)
                dve.tensor_scalar(up_c[:, :], psf[:, D:2 * D], LIMIT, -LIMIT, ALU.min, ALU.max).then_inc(up_ok, 1)

            def products(b):
                dve.wait_ge(up_ok, b + 1)
                dve.scalar_tensor_tensor(out=up_c[:, :], in0=up_c[:, :], scalar=1.0, in1=gate_c[:, :],
                                         op0=ALU.add, op1=ALU.mult).then_inc(ug_ok, 1)
                dve.wait_ge(ug_ok, b + 1)
                dve.wait_ge(sg_ok, b + 1)
                if not isinstance(b, int) or b >= 1:
                    dve.wait_ge(hid_turned, b)
                dve.tensor_tensor(hid[:, :], up_c[:, :], sig[:, :], ALU.mult).then_inc(hid_ok, 1)

            n_mid = dve.value_load(expert_of[0:1, MAXB:MAXB + 1], min_val=E - 2, max_val=MAXB - 3)
            nblk = n_mid + 2
            x_lo(0)
            for c_ in range(NSPL, W1C):
                lo_expert(0, c_)
            dve.wait_ge(chunk_used, used_up_to(0, W1C - 1))
            x_lo(1)
            clamps(0)
            products(0)

            def step_of(i):
                lo_expert(i, 0 - W2C)
                lo_expert(i, 1 - W2C)
                hidden_lo(i - 1)
                for k in range(2, 11):
                    lo_expert(i, k - W2C)
                dve.wait_ge(chunk_used, used_up_to(i, W1C - 1 - W2C))
                x_lo(i + 1)
                clamps(i)
                lo_expert(i, 11 - W2C)
                products(i)

            with dve.Fori(1, nblk) as i:
                step_of(i)
            hidden_lo(n_mid + 1)
            for k in range(W2C):
                lo_expert(nblk, k - W2C)

            dve.wait_ge(end_in, 32)
            step(dve.tensor_tensor(gate_end[:, :], gate_end[:, :], g_end[:, :], ALU.mult))
            def finish(t):
                dve.wait_ge(squares, NT + t + 1)
                dve.tensor_scalar(small[:, 64 + t:65 + t], small[:, 60 + t:61 + t], 1.0 / D, EPS, ALU.mult,
                                  ALU.add).then_inc(mean_sq, 1)
                root(64 + t, 1, rooted, 2 + t)
                dve.scalar_tensor_tensor(out=o_rows[:, t, :], in0=ff[:, t, :], scalar=small[:, 72 + t:73 + t],
                                         in1=gate_end[:, :], op0=ALU.mult, op1=ALU.mult).then_inc(normed, 1)

            for t in range(NT):
                dve.wait_ge(g_in[t], 16 * TOPK)
                step(dve.tensor_scalar(ff[:, t, :], g_buf[:, t * TOPK, :], w4[:, 0, t:t + 1], None, ALU.mult))
                for k in range(1, TOPK):
                    ins = dve.scalar_tensor_tensor(out=ff[:, t, :], in0=g_buf[:, t * TOPK + k, :],
                                                   scalar=w4[:, k, t:t + 1], in1=ff[:, t, :],
                                                   op0=ALU.mult, op1=ALU.add)
                    if k < TOPK - 1:
                        step(ins)
                ins.then_inc(ff_ok, 1)
                if t >= 1:
                    finish(t - 1)
            finish(NT - 1)

        @block.tensor
        def _(pe):
            mm = pe.matmul

            def three(out_, a_hi, a_lo, b_hi, b_lo, start, stop):
                mm(out_, a_hi, b_hi, start=start, stop=False, skip_group_check=True)
                mm(out_, a_hi, b_lo, start=False, stop=False, skip_group_check=True)
                return mm(out_, a_lo, b_hi, start=False, stop=stop, skip_group_check=True)

            pe.wait_ge(consts, 4)
            for t in range(NT):
                pe.wait_ge(xn_ok, t + 1)
                for k in range(KT):
                    ins = pe.transpose(ps[:, 2 * t + k // 4, (k % 4) * P:(k % 4 + 1) * P],
                                       x_in[:, t, k * P:(k + 1) * P], ident[:, :])
                ins.then_inc(xn_turned, 1)
            pe.wait_ge(chunk_read, KT)
            pe.wait_ge(xT_ok, 3)
            for n in range(2 * KT):
                ins = mm(ps[:, 4, n:n + 1], mod_acc[:, 0, n * P:(n + 1) * P], ones[:, 0:1], start=True, stop=True,
                         skip_group_check=True)
            ins.then_inc(mod_out, 1)

            def last_job(j):
                for b in range(4):
                    for c_ in range(2):
                        m = job_chunks(j) + c_
                        pe.wait_ge(hi_ready, m + 1)
                        pe.wait_ge(chunk_read, N_RAW1 - 1 + c_)
                        wh = w_hi[:, m % NSPL, :].rearrange("p (k n) -> p k n", k=4)
                        wl = w_lo[:, m % NSPL, :].rearrange("p (k n) -> p k n", k=4)
                        for k4 in range(4):
                            k, cols = c_ * 4 + k4, slice(b * P, (b + 1) * P)
                            ins = three(ps[:, out_bank(j, b), :], hT_hi[:, k, cols], hT_lo[:, k, cols],
                                        wh[:, k4, :], wl[:, k4, :], k == 0, k == KT - 1)
                    ins.then_inc(out_done, 1)
                pe.wait_ge(out_done, 4)
                pe.sem_inc(chunk_used, 2)

            def job(j):
                name, _, _, kt, turned = JOBS[j]
                act_hi, act_lo = {"y_sb": (o_sb_hi, o_sb_lo), "y_ca": (o_ca_hi, o_ca_lo)}.get(name, (hT_hi, hT_lo))
                for c_ in range(kt // 4):
                    m = job_chunks(j) + c_
                    pe.wait_ge(hi_ready, m + 1)
                    n_raw = [n for n, s in enumerate(STREAM) if s == ("w", j, c_)][0]
                    pe.wait_ge(chunk_read, n_raw + 1)
                    if j == N_PROJ + N_MERGE:
                        pe.wait_ge(mix_lo_ok, c_ + 1)
                    wh = w_hi[:, m % NSPL, :].rearrange("p (k n) -> p k n", k=4)
                    wl = w_lo[:, m % NSPL, :].rearrange("p (k n) -> p k n", k=4)
                    for b in range(4):
                        out_ = ps[:, out_bank(j, b), :]
                        if j == N_PROJ + N_MERGE and c_ == 0 and b == 2:
                            pe.wait_ge(y_taken, 4)
                        cols = slice(b * P, (b + 1) * P)
                        for k4 in range(4):
                            k = c_ * 4 + k4
                            if j == 0 and b == 0:
                                pe.wait_ge(hT_lo_ok, k + 1)
                            first, last_ = k == 0, k == kt - 1
                            if turned:
                                ins = three(out_, wh[:, k4, cols], wl[:, k4, cols], act_hi[:, k, :],
                                            act_lo[:, k, :], first, last_)
                            else:
                                ins = three(out_, act_hi[:, k, cols], act_lo[:, k, cols], wh[:, k4, :],
                                            wl[:, k4, :], first, last_)
                    ins.then_inc(chunk_used, 1)

            for j in range(N_PROJ):
                if j >= 2:
                    pe.wait_ge(proj_taken, j - 1)
                job(j)
            pe.wait_ge(proj_taken, N_PROJ - 1)
            pe.wait_ge(chunk_read, N_ADA_END)
            for n in range(4 * KT):
                ins = mm(ps[:, 3, n:n + 1], mod_acc[:, 1 + n // (2 * KT), (n % (2 * KT)) * P:(n % (2 * KT) + 1) * P],
                         ones[:, 0:1], start=True, stop=True, skip_group_check=True)
            ins.then_inc(mod_out, 1)

            pe.wait_ge(const_r, 2)

            def attend_ca(h):
                r = DH - DH * (h % 2)
                pe.wait_ge(pT_ok, h + 1)
                if h == 0:
                    pe.wait_ge(mod_taken, 2)
                else:
                    pe.wait_ge(os_taken, h)
                for i in range(NT):
                    ins = mm(ps[r:r + DH, 6, i * P:S], v_ca[:, i, h * DH:(h + 1) * DH],
                             pT[:, SOFF[i]:SOFF[i] + SWID[i]], start=i == 0, stop=i == NT - 1,
                             skip_group_check=True)
                ins.then_inc(oc_ok, 1)

            def attend_sb(h):
                r = DH * (h % 2)
                pe.wait_ge(a_ok, h + 1)
                if h >= 1:
                    pe.wait_ge(oc_taken, h)
                for i in range(NT):
                    ins = mm(ps[r:r + DH, 6, i * P:S], v_sb[:, i, h * DH:(h + 1) * DH],
                             stick[:, SOFF[i]:SOFF[i] + SWID[i]], start=i == 0, stop=i == NT - 1,
                             skip_group_check=True)
                ins.then_inc(os_ok, 1)

            def gate_beside(h):
                j, b = N_PROJ + h // 4, h % 4
                if h >= 1:
                    pe.wait_ge(pre_taken, h)
                cols = slice(b * P, (b + 1) * P)
                for c_ in range(2):
                    m = job_chunks(j) + c_
                    pe.wait_ge(hi_ready, m + 1)
                    pe.wait_ge(chunk_read, raw_chunks(j)[c_][0] + 1)
                    wh = w_hi[:, m % NSPL, :].rearrange("p (k n) -> p k n", k=4)
                    wl = w_lo[:, m % NSPL, :].rearrange("p (k n) -> p k n", k=4)
                    for k4 in range(4):
                        k = c_ * 4 + k4
                        ins = three(ps[:, 7, :], wh[:, k4, cols], wl[:, k4, cols], hT_hi[:, k, :], hT_lo[:, k, :],
                                    k == 0, k == KT - 1)
                ins.then_inc(pre_ok, 1)
                if b == 3:
                    pe.wait_ge(pre_ok, h + 1)
                    pe.sem_inc(chunk_used, 2)

            for h in range(HEADS):
                r, p = slice(DH * (h % 2), DH * (h % 2) + DH), h // 2
                if h >= 1:
                    pe.wait_ge(a_ok, h)
                for i in range(NT):
                    a, n = SOFF[i], SWID[i]
                    mm(psf[:, a:a + n], k_sb[r, p, i * P:(i + 1) * P], q_sb[r, p, i * P:S],
                       start=i < 3, stop=False, skip_group_check=True)
                    ins = mm(psf[:, a:a + P], ident_b[:, :], mask_b[:, :], start=False, stop=False,
                             skip_group_check=True)
                ins.then_inc(zs_ok, 1)
                if h >= 1:
                    attend_ca(h - 1)
                    attend_sb(h - 1)
                else:
                    pe.wait_ge(proj_taken, N_PROJ)
                    pe.wait_ge(mod_taken, 1)
                    pe.transpose(ps[0:4 * KT, 6, 0:P], mod_col[:, :], ident[:, :]).then_inc(mod_turned, 1)
                for i in (3, 2, 1, 0):
                    a, n = 1536 + QOFF[i], QWID[i]
                    ins = mm(psf[:, a:a + n], q_ca[r, p, i * P:(i + 1) * P], k_ca[r, p, 0:n],
                             start=i > 0, stop=True, skip_group_check=True)
                ins.then_inc(zc_ok, 1)
                gate_beside(h)
                pe.wait_ge(sp_hi_ok, h + 1)
                pe.wait_ge(sp_lo_ok, h + 1)
                for i in range(NT):
                    for j in range(i, NT):
                        o = SOFF[i] + P * (j - i)
                        for part in (sp_hi, sp_lo):
                            ins = mm(psf[:, o:o + SWID[j]], neg_tri[:, :] if j == i else neg_ones[:, :],
                                     part[:, SOFF[j]:SOFF[j] + SWID[j]], start=False,
                                     stop=(part is sp_lo and j == NT - 1), skip_group_check=True)
                ins.then_inc(stick_ok, 1)
                pe.wait_ge(p_ok, h + 1)
                for j in range(NT):
                    for i in range(j, NT):
                        o = 1536 + SOFF[j] + P * (i - j)
                        q = QOFF[i] + j * P
                        ins = pe.transpose(psf[:, o:o + P], zb[:, q:q + P], ident[:, :])
                ins.then_inc(p_turned, 1)
            attend_ca(HEADS - 1)
            attend_sb(HEADS - 1)

            first = N_PROJ + N_BESIDE
            job(first)
            pe.wait_ge(os_taken, HEADS)
            pe.wait_ge(oc_taken, HEADS)
            pe.wait_ge(pre_taken, HEADS)
            pe.wait_ge(o_lo_ok, 1)
            job(first + 1)
            pe.wait_ge(gate_taken, 1)
            job(first + 2)
            pe.wait_ge(y_taken, 1)
            pe.wait_ge(o_lo_ok, 2)
            job(first + 3)
            pe.wait_ge(y_taken, 2)
            job(first + 4)
            pe.wait_ge(y_taken, 3)
            job(first + 5)
            pe.wait_ge(gate_taken, 2)
            job(N_PROJ + N_MERGE)
            last_job(N_PROJ + N_MERGE + 1)

            def turn_h2(t):
                pe.wait_ge(h2_ok, t + 1)
                for k in range(KT):
                    ins = pe.transpose(ps[:, 2 * t + k // 4, (k % 4) * P:(k % 4 + 1) * P],
                                       h2[:, t, k * P:(k + 1) * P], ident[:, :])
                ins.then_inc(h2_turned, 1)

            def logits(t):
                pe.wait_ge(h2T_ok, t + 1)
                cols = slice(t * P, (t + 1) * P)
                mm(ps[0:E, 0, cols], br[0:1, :], ones[0:1, :], start=True, stop=False, skip_group_check=True)
                for k in range(KT):
                    ins = mm(ps[0:E, 0, cols], wr[:, k, :], h2T[:, k, cols], start=False, stop=k == KT - 1,
                             skip_group_check=True)
                return ins

            turn_h2(0)
            turn_h2(1)
            pe.wait_ge(router_in, 32)
            logits(0)
            for t in range(2, NT):
                turn_h2(t)
                logits(t - 1)
            logits(NT - 1).then_inc(logits_ok, 1)
            pe.wait_ge(logit_t_ok, 1)
            for t in range(NT):
                ins = pe.transpose(ps[:, 4, t * E:(t + 1) * E], logit_t[:, t * P:(t + 1) * P], ident[0:E, 0:E])
            ins.then_inc(logits_back, 1)
            pe.wait_ge(consts, 11)
            pe.wait_ge(mask_ok, 1)
            for t in range(NT):
                mm(ps[:, 5, t * E:(t + 1) * E], tri[:, :], r_mask[:, t, :], start=True, stop=t == 0)
                for u in range(t):
                    mm(ps[:, 5, t * E:(t + 1) * E], ones_b[:, :], r_mask[:, u, :], start=False, stop=u == t - 1)
            for t in range(NT):
                ins = mm(ps[:, 6, 0:E], ones_b[:, :], r_mask[:, t, :], start=t == 0, stop=t == NT - 1)
            ins.then_inc(rank_ok, 1)
            for n in range(NT * TOPK):
                pe.wait_ge(hot_ok, n // TOPK + 1)
                ins = mm(ps[:, 7, 0:MAXB], hot_r[:, n, :], hot_n[:, n, :], start=n == 0, stop=n == NT * TOPK - 1)
            ins.then_inc(hot_used, 1)

            def turn(src):
                for k in range(KT):
                    ins = pe.transpose(ps[:, 6 + k // 4, (k % 4) * P:(k % 4 + 1) * P], src[:, k * P:(k + 1) * P],
                                       ident[:, :])
                return ins

            def w_chunk(i, q, bank0, banks, a_hi, a_lo, ktiles, width, last_):
                pe.wait_ge(hi_ready, used_up_to(i, q))
                pe.wait_ge(chunk_read, read_up_to(i, q))
                hi, lo = his[spl_slot(q)], los[spl_slot(q)]
                for n, k in enumerate(ktiles):
                    for a, w in ((a_hi, hi), (a_hi, lo), (a_lo, hi)):
                        for b in range(banks):
                            o = n * width + b * 512
                            ins = mm(ps[:, bank0 + b, :], a[:, k, :], w[:, o:o + 512], start=False,
                                     stop=last_ and k == ktiles[-1] and a is a_lo, skip_group_check=True)
                ins.then_inc(chunk_used, 1)

            def w1_run(b):
                w1_start(b)
                for c_ in range(W1C):
                    w_chunk(b, c_ if isinstance(b, int) and b == 0 else c_ - W2C, 0, 4, xT_hi, xT_lo, (c_,), 0,
                            c_ == W1C - 1)

            def w1_start(b):
                pe.wait_ge(b1_in, b * 16 + 16)
                pe.wait_ge(xT_lo_ok, b + 1)
                if not isinstance(b, int) or b >= 1:
                    pe.wait_ge(up_ok, b)
                for n in range(4):
                    ins = mm(ps[:, n, :], ones_r[:, :], brow1[:, n * 512:(n + 1) * 512], start=True, stop=False,
                             skip_group_check=True)
                ins.then_inc(b1_used, 1)

            def w2_start(b):
                pe.wait_ge(b2_in, b * 16 + 16)
                pe.wait_ge(hidT_lo_ok, b + 1)
                if not isinstance(b, int) or b >= 1:
                    pe.wait_ge(y_ok, b)
                for n in range(2):
                    ins = mm(ps[:, 4 + n, :], ones_r[:, :], brow2[:, n * 512:(n + 1) * 512], start=True, stop=False,
                             skip_group_check=True)
                ins.then_inc(b2_used, 1)

            def w2_run(b, i, q0):
                w2_start(b)
                for c_ in range(W2C):
                    w_chunk(i, q0 + c_, 4, 2, hidT_hi, hidT_lo, (2 * c_, 2 * c_ + 1), D, c_ == W2C - 1)

            def turn_x(b):
                pe.wait_ge(x_gathered, b * 16 + 16)
                if not isinstance(b, int) or b >= 2:
                    pe.wait_ge(hidT_lo_ok, b - 1)
                elif b == 1:
                    pe.wait_ge(xT_lo_ok, 1)
                turn(x_rows).then_inc(x_turned, 1)

            def turn_hidden(b):
                pe.wait_ge(hid_ok, b + 1)
                pe.wait_ge(xT_lo_ok, b + 2)
                turn(hid).then_inc(hid_turned, 1)

            pe.wait_ge(table_ok, 1)
            n_mid = pe.value_load(expert_of[0:1, MAXB:MAXB + 1], min_val=E - 2, max_val=MAXB - 3)
            nblk = n_mid + 2
            pe.wait_ge(const_r, 3)
            turn_x(0)
            w1_run(0)
            turn_x(1)
            turn_hidden(0)

            def step_of(i):
                w1_run(i)
                turn_x(i + 1)
                w2_run(i - 1, i, W1C - W2C)
                turn_hidden(i)

            step_of(1)
            with pe.Fori(2, nblk) as i:
                step_of(i)
            w2_run(n_mid + 1, nblk, -W2C)


_INS = ["x", "c", "w_ada", "b_ada", "g_pre_mix", "g_post_mix", "w_in", "rel_bias", "w_branch_sb", "w_branch_ca",
        "w_gate", "b_gate", "w_out", "g_pre_ffn", "g_post_ffn", "w_router", "b_router", "w_e1", "b_e1", "w_e2",
        "b_e2"]


def kernel(**inputs):
    import numpy as np
    import concourse.bacc as bacc
    from concourse.bass_utils import run_bass_kernel_spmd

    nc = bacc.Bacc("TRN2", target_bir_lowering=False, num_devices=1)
    arrays, args = {}, []
    for name in _INS:
        a = np.asarray(inputs[name])
        if name == "rel_bias":
            at = np.arange(P)[:, None] + (S - P) - np.arange(S)[None, :]
            a = a[0][:, np.clip(at, -REL_CLIP, REL_CLIP) + REL_CLIP]
        a = np.ascontiguousarray(a)
        arrays[f"in_{name}"] = a
        args.append(nc.dram_tensor(f"in_{name}", a.shape, mybir.dt.from_np(a.dtype), kind="ExternalInput").ap())
    args.append(nc.dram_tensor("out_x", (1, S, D), F32, kind="ExternalOutput").ap())
    trunk_layer(nc, *args)
    r = run_bass_kernel_spmd(nc, [arrays], core_ids=[0])
    return r.results[0]["out_x"]
```
